# Optimizing a Trainium2 kernel written in Bass

```python
import math
import jax, jax.numpy as jnp
from jax import lax
import numpy as np

D_MODEL = 2048
BATCH = 1
SEQ = 256
DEPTH = 1

HEAD_DIM = 128
N_HEADS_SB = 8
N_HEADS_MOBA = 8
W_SB = N_HEADS_SB * HEAD_DIM
W_MOBA = N_HEADS_MOBA * HEAD_DIM
W_MIX = W_SB + W_MOBA
SB_BLOCK = 128
MOBA_BLOCK = 256
MOBA_TOP_K = 3
MOBA_Q_CHUNK = 16
ROPE_DIM = HEAD_DIM // 4
ROPE_THETA = 500000.0
N_MEM = 256
N_HEADS_X = 4
W_X = N_HEADS_X * HEAD_DIM
D_FF = ((8 * D_MODEL + 3 * 256 - 1) // (3 * 256)) * 256
EPS = 1e-6
ATTN_SCALE = HEAD_DIM ** -0.5

kernel_name = "hybrid_stickbreak_moba_memxattn_swiglu"

def rmsnorm(x, g):
    xf = x.astype(jnp.float32)
    y = xf * lax.rsqrt(jnp.mean(xf * xf, axis=-1, keepdims=True) + EPS)
    return (y * g.astype(jnp.float32)).astype(x.dtype)

def partial_rotary(x, positions):
    half = ROPE_DIM // 2
    inv_freq = ROPE_THETA ** (-jnp.arange(0, ROPE_DIM, 2, dtype=jnp.float32) / ROPE_DIM)
    ang = positions.astype(jnp.float32)[:, None, :, None] * inv_freq
    cos, sin = jnp.cos(ang), jnp.sin(ang)
    xf = x.astype(jnp.float32)
    x1, x2, rest = xf[..., :half], xf[..., half:ROPE_DIM], xf[..., ROPE_DIM:]
    out = jnp.concatenate([x1 * cos - x2 * sin, x2 * cos + x1 * sin, rest], axis=-1)
    return out.astype(x.dtype)

def stick_breaking_attention(q, k, v):
    S = q.shape[2]
    outs = []
    for i in range(S // SB_BLOCK):
        t0, t1 = i * SB_BLOCK, (i + 1) * SB_BLOCK
        qb = q[:, :, t0:t1].astype(jnp.float32)
        kb = k[:, :, :t1].astype(jnp.float32)
        vb = v[:, :, :t1]
        z = jnp.einsum('bhtd,bhsd->bhts', qb, kb) * ATTN_SCALE
        t_pos = t0 + jnp.arange(SB_BLOCK)[:, None]
        s_pos = jnp.arange(t1)[None, :]
        past = s_pos < t_pos
        log_1m_beta = jnp.where(past, jax.nn.log_sigmoid(-z), 0.0)
        after = lax.cumsum(log_1m_beta, axis=3, reverse=True) - log_1m_beta
        w = jnp.where(past, jnp.exp(jax.nn.log_sigmoid(z) + after), 0.0)
        outs.append(jnp.einsum('bhts,bhsd->bhtd', w.astype(vb.dtype), vb))
    return jnp.concatenate(outs, axis=2)

def moba_attention(q, k, v):
    B, H, S, d = q.shape
    NB = -(-S // MOBA_BLOCK)
    pad = NB * MOBA_BLOCK - S
    kp = jnp.pad(k, ((0, 0), (0, 0), (0, pad), (0, 0)))
    vp = jnp.pad(v, ((0, 0), (0, 0), (0, pad), (0, 0)))
    kblk = kp.reshape(B, H, NB, MOBA_BLOCK, d)
    vblk = vp.reshape(B, H, NB, MOBA_BLOCK, d)
    kmean = jnp.mean(kblk.astype(jnp.float32), axis=3)
    n_sel = min(MOBA_TOP_K, NB)
    bi = jnp.arange(B)[:, None, None, None]
    hi = jnp.arange(H)[None, :, None, None]

    def chunk(ci):
        t0 = ci * MOBA_Q_CHUNK
        blk = t0 // MOBA_BLOCK
        qc = lax.dynamic_slice_in_dim(q, t0, MOBA_Q_CHUNK, axis=2).astype(jnp.float32)
        gate = jnp.einsum('bhqd,bhnd->bhqn', qc, kmean)
        fully_past = jnp.arange(NB) < blk
        gate = jnp.where(fully_past, gate, -jnp.inf)
        top_val, top_idx = lax.top_k(gate, n_sel)
        valid = jnp.isfinite(top_val)
        kg = kblk[bi, hi, top_idx]
        vg = vblk[bi, hi, top_idx]
        s_sel = jnp.einsum('bhqd,bhqncd->bhqnc', qc, kg.astype(jnp.float32)) * ATTN_SCALE
        s_sel = jnp.where(valid[..., None], s_sel, -jnp.inf)
        s_sel = s_sel.reshape(B, H, MOBA_Q_CHUNK, n_sel * MOBA_BLOCK)
        k_own = lax.dynamic_slice_in_dim(kp, blk * MOBA_BLOCK, MOBA_BLOCK, axis=2)
        v_own = lax.dynamic_slice_in_dim(vp, blk * MOBA_BLOCK, MOBA_BLOCK, axis=2)
        s_own = jnp.einsum('bhqd,bhcd->bhqc', qc, k_own.astype(jnp.float32)) * ATTN_SCALE
        key_pos = blk * MOBA_BLOCK + jnp.arange(MOBA_BLOCK)
        q_pos = t0 + jnp.arange(MOBA_Q_CHUNK)
        s_own = jnp.where(key_pos[None, :] <= q_pos[:, None], s_own, -jnp.inf)
        p = jax.nn.softmax(jnp.concatenate([s_sel, s_own], axis=-1), axis=-1)
        p_sel = p[..., :n_sel * MOBA_BLOCK].reshape(B, H, MOBA_Q_CHUNK, n_sel, MOBA_BLOCK)
        p_own = p[..., n_sel * MOBA_BLOCK:]
        return (jnp.einsum('bhqnc,bhqncd->bhqd', p_sel.astype(v.dtype), vg)
                + jnp.einsum('bhqc,bhcd->bhqd', p_own.astype(v.dtype), v_own))

    outs = lax.map(chunk, jnp.arange(S // MOBA_Q_CHUNK))
    return outs.transpose(1, 2, 0, 3, 4).reshape(B, H, S, d)

def split_heads(t, n_heads):
    B, S, _ = t.shape
    return t.reshape(B, S, n_heads, HEAD_DIM).transpose(0, 2, 1, 3)

def parallel_mixer(h, positions, w_in, g_out_sb, g_out_moba, w_out):
    B, S, _ = h.shape
    proj = h @ w_in
    q_sb, k_sb, v_sb, q_mb, k_mb, v_mb = jnp.split(
        proj, [W_SB, 2 * W_SB, 3 * W_SB, 3 * W_SB + W_MOBA, 3 * W_SB + 2 * W_MOBA], axis=-1)
    o_sb = stick_breaking_attention(split_heads(q_sb, N_HEADS_SB),
                                    split_heads(k_sb, N_HEADS_SB),
                                    split_heads(v_sb, N_HEADS_SB))
    q_mb = partial_rotary(split_heads(q_mb, N_HEADS_MOBA), positions)
    k_mb = partial_rotary(split_heads(k_mb, N_HEADS_MOBA), positions)
    o_mb = moba_attention(q_mb, k_mb, split_heads(v_mb, N_HEADS_MOBA))
    o_sb = rmsnorm(o_sb.transpose(0, 2, 1, 3), g_out_sb.reshape(N_HEADS_SB, HEAD_DIM))
    o_mb = rmsnorm(o_mb.transpose(0, 2, 1, 3), g_out_moba.reshape(N_HEADS_MOBA, HEAD_DIM))
    o = jnp.concatenate([o_sb.reshape(B, S, W_SB), o_mb.reshape(B, S, W_MOBA)], axis=-1)
    return o @ w_out

def memory_cross_attention(h, m, w_xq, w_xkv, w_xo):
    B, S, _ = h.shape
    q = split_heads(h @ w_xq, N_HEADS_X).astype(jnp.float32)
    kv = (m @ w_xkv).reshape(B, N_MEM, 2, N_HEADS_X, HEAD_DIM)
    k = kv[:, :, 0].transpose(0, 2, 1, 3)
    v = kv[:, :, 1].transpose(0, 2, 1, 3)
    s = jnp.einsum('bhsd,bhmd->bhsm', q, k.astype(jnp.float32)) * ATTN_SCALE
    p = jax.nn.softmax(s, axis=-1)
    o = jnp.einsum('bhsm,bhmd->bhsd', p.astype(v.dtype), v)
    return o.transpose(0, 2, 1, 3).reshape(B, S, W_X) @ w_xo

def swiglu(h, w_gate_up, w_down):
    gu = h @ w_gate_up
    g, u = jnp.split(gu, 2, axis=-1)
    return (jax.nn.silu(g) * u) @ w_down

def setup_inputs(seed: int = 0) -> dict:
    key = jax.random.key(seed)
    ks = jax.random.split(key, 16)

    def w(k, fan_in, fan_out):
        return jax.random.normal(k, (fan_in, fan_out), jnp.float32) * fan_in ** -0.5

    def gain(k, n):
        return 1.0 + 0.01 * jax.random.normal(k, (n,), jnp.float32)

    x = jax.random.normal(ks[0], (BATCH, SEQ, D_MODEL), jnp.float32)
    mem = jax.random.normal(ks[1], (BATCH, N_MEM, D_MODEL), jnp.float32)
    offset = jax.random.randint(ks[2], (BATCH, 1), 0, 4096, dtype=jnp.int32)
    positions = offset + jnp.arange(SEQ, dtype=jnp.int32)[None, :]
    return {
        "x": x,
        "mem": mem,
        "positions": positions,
        "g_mix": gain(ks[3], D_MODEL),
        "w_in": w(ks[4], D_MODEL, 3 * W_SB + 3 * W_MOBA),
        "g_out_sb": gain(ks[5], W_SB),
        "g_out_moba": gain(ks[6], W_MOBA),
        "w_out": w(ks[7], W_MIX, D_MODEL),
        "g_xattn": gain(ks[8], D_MODEL),
        "g_mem": gain(ks[9], D_MODEL),
        "w_xq": w(ks[10], D_MODEL, W_X),
        "w_xkv": w(ks[11], D_MODEL, 2 * W_X),
        "w_xo": w(ks[12], W_X, D_MODEL),
        "g_ffn": gain(ks[13], D_MODEL),
        "w_gate_up": w(ks[14], D_MODEL, 2 * D_FF),
        "w_down": w(ks[15], D_FF, D_MODEL),
        "g_final": gain(jax.random.fold_in(key, 99), D_MODEL),
    }

def reference(x, mem, positions, g_mix, w_in, g_out_sb, g_out_moba, w_out,
              g_xattn, g_mem, w_xq, w_xkv, w_xo, g_ffn, w_gate_up, w_down, g_final):
    m = rmsnorm(mem, g_mem)
    for _ in range(DEPTH):
        x = x + parallel_mixer(rmsnorm(x, g_mix), positions, w_in, g_out_sb, g_out_moba, w_out)
        x = x + memory_cross_attention(rmsnorm(x, g_xattn), m, w_xq, w_xkv, w_xo)
        x = x + swiglu(rmsnorm(x, g_ffn), w_gate_up, w_down)
    return rmsnorm(x, g_final)


_drawn_inputs = setup_inputs


def setup_inputs(seed=0):
    import zlib

    import numpy as np

    out = dict(_drawn_inputs(seed))
    spreads = {}
    factors = {'g_mix': 5.329,
     'g_out_sb': 8.0,
     'g_out_moba': 8.0,
     'g_xattn': 8.0,
     'g_mem': 8.0,
     'g_ffn': 8.0,
     'g_final': 5.694}
    for name, (base, spread) in spreads.items():
        noise = np.random.default_rng([zlib.crc32(name.encode()), seed]).standard_normal(out[name].shape)
        drawn = base * np.exp(spread * noise) if base else spread * noise
        out[name] = __import__('jax').numpy.asarray(drawn.astype(out[name].dtype))
    for name, factor in factors.items():
        out[name] = (out[name] * factor).astype(out[name].dtype)
    return out
```

```python
from contextlib import ExitStack

import numpy as np

import concourse.bass as bass
from concourse import mybir
from concourse.alu_op_type import AluOpType as ALU

F32 = mybir.dt.float32
F32R = mybir.dt.float32r
I32 = mybir.dt.int32
ACT = mybir.ActivationFunctionType
AX = mybir.AxisListType

P = 128
D = 2048
S = 256
HALVES = S // P
N_MEM = 256
HD = 128
W_GROUP = 512
HEADS = W_GROUP // HD
N_SB, N_MB = 8, 8
W_SB, W_MB = N_SB * HD, N_MB * HD
ROPE = HD // 4
RHALF = ROPE // 2
THETA = 500000.0
D_FF = ((8 * D + 3 * 256 - 1) // (3 * 256)) * 256
EPS = 1e-6
SCALE = HD ** -0.5
MASKED = -1e30

KT = D // P
PIECE = 1024
SLOTS = 4
CP = KT * W_GROUP // PIECE
TG = D // W_GROUP
LEAD = 2
GROUPS = W_SB // W_GROUP
FC = D_FF // W_GROUP
FK = D_FF // P
XP = W_GROUP * W_GROUP // P // PIECE

MIX_STEP = 7 * CP
P_WOUT = GROUPS * MIX_STEP
P_XQ = P_WOUT + TG * CP
P_XO = P_XQ + CP
P_GATE0 = P_XO + TG * XP
P_FFN = P_GATE0 + CP
P_DOWN = P_FFN + (2 * FC - 1) * CP
P_END = P_DOWN + 2 * FK
DOWN_STEP = 2 * SLOTS

T_MEM = TG
T_MIX = T_MEM + TG
T_O = T_MIX + 4 * GROUPS
T_KX = T_O + TG
T_WOUT = T_KX + 1
T_XO = T_WOUT + TG
T_H = T_XO + TG
T_END = T_H + FC

SPLIT_X, SPLIT_MEM, SPLIT_O, SPLIT_WOUT, SPLIT_XO = (TG * n for n in range(5))

NORM_X, NORM_MEM, NORM_HEADS = 0, 1, 2
NORM_Q = NORM_HEADS + 2 * GROUPS
NORM_F = NORM_Q + 1
NORM_OUT = NORM_F + 1

XQ_PIECES = [(0, 0), (1, 0), (0, 1), (1, 1), (2, 0), (2, 1), (3, 0), (3, 1)]
XO_PIECES = [(0, 0), (1, 0), (0, 1), (1, 1), (2, 0), (2, 1), (3, 0), (3, 1)]

G_MIX, G_MEM, G_X, G_FFN = 0, KT, 2 * KT, 3 * KT
G_O = 4 * KT
G_ROWS = G_O + KT

TRIG_STEPS = (2.0 ** 20, 2.0 ** 10, 1.0)


def split_two_pi():
    hi, lo = 6.283185307179586, 2.4492935982947064e-16
    parts, rest = [], hi
    for n in range(4):
        unit = 2.0 ** (2 - 11 * (n + 1))
        part = float(np.floor(rest / unit) * unit)
        parts.append(part)
        rest -= part
    return parts + [rest + lo]


class Chain:

    def __init__(self, engine, done, base=0):
        self.engine, self.done, self.base, self.n = engine, done, base, 0

    def __call__(self, instruction):
        self.n += 1
        instruction.then_inc(self.done, 1)
        self.engine.wait_ge(self.done, self.base + self.n)

    def at(self, base):
        self.base, self.n = base, 0


def build(nc, x, mem, positions, g_mix, w_in, g_out_sb, g_out_moba, w_out, g_xattn, g_mem,
          w_xq, w_xkv, w_xo, g_ffn, w_gate_up, w_down, g_final, out):
    place = [(nc.sbuf_base + 31) // 32 * 32]

    def sb(name, shape, dtype=F32, at=None):
        size = 4 * int(np.prod(shape[1:]))
        size = (size + 31) // 32 * 32
        if at is None:
            at = place[0]
            place[0] += size
            assert place[0] <= nc.sbuf_usable_end, (name, place[0])
        return nc.alloc_sbuf_tensor_at(name, shape, dtype, offset=at)

    x_tok = sb("x_tok", [P, HALVES, D])
    w_raw = sb("w_raw", [P, SLOTS, PIECE])
    w_hi = sb("w_hi", [P, SLOTS, PIECE], F32R)
    w_lo = sb("w_lo", [P, SLOTS, PIECE], F32R)
    t1_hi = sb("t1_hi", [P, KT, S], F32R)
    t1_lo = sb("t1_lo", [P, KT, S], F32R)
    t0_at = place[0]
    t0_hi = sb("t0_hi", [P, KT, S], F32R)
    t0_lo = sb("t0_lo", [P, KT, S], F32R)
    o_tok = sb("o_tok", [P, HALVES, D])
    hT = sb("hT", [P, FK, S], at=t0_at)
    assert t0_at + FK * S * 4 <= place[0]
    qkv_at = place[0]
    qT = sb("qT", [P, 2, HEADS, S])
    kT = sb("kT", [P, 2, HEADS, S])
    v_tok = sb("v_tok", [P, 2, HALVES, W_GROUP])
    h_hi = sb("h_hi", [P, SLOTS, S], F32R, at=qkv_at)
    h_lo = sb("h_lo", [P, SLOTS, S], F32R, at=qkv_at + SLOTS * S * 4)
    gfin = sb("gfin", [P, D], at=qkv_at + 2 * SLOTS * S * 4)
    qk_tok = sb("qk_tok", [P, 2, HALVES, W_GROUP])
    kvx_tok = sb("kvx_tok", [P, 2, HALVES, W_GROUP])
    s_a = sb("s_a", [P, 2, W_GROUP])
    s_b = sb("s_b", [P, 2, W_GROUP])
    s_c = sb("s_c", [P, 2, W_GROUP])
    ident = sb("ident", [P, P])
    neg_tri = sb("neg_tri", [P, P])
    neg_one = sb("neg_one", [P, P])
    causal = sb("causal", [P, 3 * P])
    past_one = sb("past_one", [P, 2 * P])
    ident_r = sb("ident_r", [P, P], F32R)
    not_past = sb("not_past", [P, 2 * P], F32R)
    g_rows = sb("g_rows", [G_ROWS, P])
    g_col = sb("g_col", [P, G_ROWS])
    pos_i = sb("pos_i", [P, HALVES], I32)
    pos_f = sb("pos_f", [P, HALVES])
    inv_freq = sb("inv_freq", [P, RHALF])
    ang = sb("ang", [P, HALVES * RHALF])
    turns = sb("turns", [P, HALVES * RHALF])
    cos_arg = sb("cos_arg", [P, HALVES * RHALF])
    sin_t = sb("sin_t", [P, HALVES, RHALF])
    cos_t = sb("cos_t", [P, HALVES, RHALF])
    rot = sb("rot", [P, 4, HALVES, HEADS * RHALF])
    ssq = sb("ssq", [P, 16])
    ms = sb("ms", [P, 8])
    ln_ms = sb("ln_ms", [P, 8])
    rs = sb("rs", [P, 8])
    nt = sb("nt", [P, 8])
    fac = sb("fac", [P, 8])
    rden = sb("rden", [P, 8])
    rowsum = sb("rowsum", [P, HALVES * HEADS])
    negmax = sb("negmax", [P, 2, HALVES])
    rstd_x = sb("rstd_x", [P, HALVES])
    rstd_m = sb("rstd_m", [P, HALVES])
    scale_q = sb("scale_q", [P, HALVES])
    rstd_f = sb("rstd_f", [P, HALVES])
    rstd_o = sb("rstd_o", [P, HALVES])
    wide = s_a[:, :, :].rearrange("p a b -> p (a b)")

    with ExitStack() as ctx:
        psum = ctx.enter_context(nc.psum_tensor("psum", [P, 8, 512], F32))

        def pair(n):
            return psum[:, 2 * n:2 * n + 2, :]

        def down_bank(hf, c):
            return psum[:, (2 * (c // 2) if hf == 0 else 6 - 2 * (c // 2)) + c % 2, :]

        def sem(name):
            return ctx.enter_context(nc.semaphore(name))

        x_landed = [sem(f"x_landed{c}") for c in range(TG)]
        mem_landed = [sem(f"mem_landed{c}") for c in range(TG)]
        gains_landed = sem("gains_landed")
        pos_landed = sem("pos_landed")
        gfin_landed = sem("gfin_landed")
        raw_landed = [sem(f"raw_landed{s}") for s in range(SLOTS)]
        hi_ready = sem("hi_ready")
        lo_ready = sem("lo_ready")
        piece_used = sem("piece_used")
        consts_ready = sem("consts_ready")
        gains_turned = sem("gains_turned")
        gains_ready = sem("gains_ready")
        t_done = sem("t_done")
        t_hi_ready = sem("t_hi_ready")
        t_out = sem("t_out")
        trig_args = sem("trig_args")
        trig_ready = sem("trig_ready")
        evac = sem("evac")
        ssq_ready = sem("ssq_ready")
        ms_ready = sem("ms_ready")
        root_ready = sem("root_ready")
        rstd_ready = sem("rstd_ready")
        rotated = sem("rotated")
        z_done = sem("z_done")
        log_ready = sem("log_ready")
        sp_ready = sem("sp_ready")
        sp_masked = sem("sp_masked")
        cum_done = sem("cum_done")
        w_exp = sem("w_exp")
        s_done = sem("s_done")
        s_out = sem("s_out")
        max_ready = sem("max_ready")
        p_ready = sem("p_ready")
        pt_done = sem("pt_done")
        pt_out = sem("pt_out")
        heads_done = sem("heads_done")
        o_out = sem("o_out")
        resid = sem("resid")
        silu_out = sem("silu_out")
        o_hi_ready = sem("o_hi_ready")
        diag_ready = sem("diag_ready")
        h_ready = sem("h_ready")
        h_hi_ready = sem("h_hi_ready")
        h_split = sem("h_split")
        bank_done = sem("bank_done")
        final_ready = sem("final_ready")
        out_written = sem("out_written")
        act_step = sem("act_step")
        dve_step = sem("dve_step")
        pool_step = sem("pool_step")

        block = ctx.enter_context(nc.Block())

        @block.sync
        def _(sp):
            def load(n, s, src):
                sp.wait_ge(lo_ready, n + 1)
                dst = w_raw[:, s, :]
                if len(src.shape) == 3:
                    dst = dst.rearrange("p (t c) -> p t c", t=src.shape[1])
                sp.dma_start(dst, src).then_inc(raw_landed[s], 16)

            def load_chunk(n, w, col, pieces=CP):
                for j in range(pieces):
                    rows = w[2 * j * P:(2 * j + 2) * P, bass.ds(col, W_GROUP)]
                    load(n + j, j % SLOTS, rows.rearrange("(t p) c -> p t c", p=P))

            for c in range(TG):
                cols = slice(c * W_GROUP, (c + 1) * W_GROUP)
                sp.dma_start(x_tok[:, :, cols], x[0, :, cols].rearrange("(h p) c -> p h c", p=P)) \
                    .then_inc(x_landed[c], 16)
            with sp.Fori(0, GROUPS) as i:
                for c in range(6):
                    load_chunk(MIX_STEP * i + c * CP, w_in, W_GROUP * i + c * W_SB)
                load_chunk(MIX_STEP * i + 6 * CP, w_xkv, W_GROUP * i)
            with sp.Fori(0, TG) as i:
                load_chunk(P_WOUT + CP * i, w_out, W_GROUP * i)
            for e, (h, half) in enumerate(XQ_PIECES):
                rows = w_xq[half * D // 2:(half + 1) * D // 2, h * HD:(h + 1) * HD]
                load(P_XQ + e, e % SLOTS, rows.rearrange("(t p) c -> p t c", p=P))
            for e, (c, half) in enumerate(XO_PIECES):
                rows = w_xo[2 * half * P:(2 * half + 2) * P, c * W_GROUP:(c + 1) * W_GROUP]
                load(P_XO + e, e % SLOTS, rows.rearrange("(t p) c -> p t c", p=P))
            load_chunk(P_GATE0, w_gate_up, 0)
            with sp.Fori(0, FC - 1) as i:
                load_chunk(P_FFN + 2 * CP * i, w_gate_up, D_FF + W_GROUP * i)
                load_chunk(P_FFN + 2 * CP * i + CP, w_gate_up, W_GROUP * i + W_GROUP)
            load_chunk(P_FFN + 2 * CP * (FC - 1), w_gate_up, 2 * D_FF - W_GROUP)
            with sp.Fori(0, FK // SLOTS) as i:
                for j in range(DOWN_STEP):
                    rows = w_down[bass.ds(SLOTS * P * i + (j // 2) * P, P),
                                  (j % 2) * PIECE:(j % 2 + 1) * PIECE]
                    load(P_DOWN + DOWN_STEP * i + j, j % SLOTS, rows)
            for hf in range(HALVES):
                for q in range(2):
                    sp.wait_ge(final_ready, 2 * hf + q + 1)
                    sp.dma_start(out[0, hf * P:(hf + 1) * P, q * PIECE:(q + 1) * PIECE],
                                 x_tok[:, hf, q * PIECE:(q + 1) * PIECE]).then_inc(out_written, 16)
            sp.wait_ge(out_written, 16 * 2 * HALVES)

        @block.gpsimd
        def _(pool):
            chain = Chain(pool, pool_step)
            for b in range(RHALF):
                pool.memset(inv_freq[:, b:b + 1], float(np.float32(THETA ** (-2.0 * b / ROPE))))
            pool.memset(neg_one[:, :], -1.0)
            pool.memset(ident[:, :], 0.0)
            pool.memset(neg_tri[:, :], -1.0)
            pool.memset(causal[:, :], 0.0)
            pool.memset(past_one[:, :], 1.0)
            chain(pool.memset(s_a[:, 0, 0:2 * P], 0.0))
            pool.affine_select(out=ident[:, :], in_=ident[:, :], compare_op=ALU.not_equal, fill=1.0,
                               base=0, pattern=[[-1, P]], channel_multiplier=1)
            pool.affine_select(out=neg_tri[:, :], in_=neg_tri[:, :], compare_op=ALU.is_ge, fill=0.0,
                               base=0, pattern=[[-1, P]], channel_multiplier=1)
            diag = causal[:, 0:2 * P].rearrange("p (b t) -> p b t", b=2)
            pool.affine_select(out=diag, in_=diag, compare_op=ALU.is_ge, fill=MASKED,
                               base=0, pattern=[[0, 2], [-1, P]], channel_multiplier=1)
            keys = [t[:, 0:2 * P].rearrange("p (b t) -> p b t", b=2)
                    for t in (past_one, s_a[:, 0, :], not_past)]
            for src, dst, fill in ((keys[0], keys[0], 0.0), (keys[1], keys[2], MASKED)):
                ins = pool.affine_select(out=dst, in_=src, compare_op=ALU.is_ge, fill=fill,
                                         base=-1, pattern=[[0, 2], [1, P]], channel_multiplier=-1)
            chain(ins)
            pool.tensor_copy(ident_r[:, :], ident[:, :]).then_inc(consts_ready, 1)

            pool.wait_ge(pos_landed, 16)
            chain(pool.tensor_copy(pos_f[:, :], pos_i[:, :]))
            for hf in range(HALVES):
                ins = pool.tensor_scalar(ang[:, hf * RHALF:(hf + 1) * RHALF], inv_freq[:, :],
                                         pos_f[:, hf:hf + 1], None, ALU.mult)
            chain(ins)
            magic = 1.5 * 2.0 ** 23
            for scale in TRIG_STEPS:
                chain(pool.tensor_scalar(turns[:, :], ang[:, :], 1.0 / (2 * np.pi * scale), None,
                                         ALU.mult))
                chain(pool.tensor_scalar(turns[:, :], turns[:, :], magic, None, ALU.add))
                chain(pool.tensor_scalar(turns[:, :], turns[:, :], -magic, None, ALU.add))
                for part in split_two_pi():
                    chain(pool.tensor_scalar(cos_arg[:, :], turns[:, :], part * scale, None,
                                             ALU.mult))
                    chain(pool.tensor_tensor(ang[:, :], ang[:, :], cos_arg[:, :], ALU.subtract))
            below_pi = 3.1415925
            chain(pool.tensor_scalar(ang[:, :], ang[:, :], below_pi, None, ALU.min))
            chain(pool.tensor_scalar(ang[:, :], ang[:, :], -below_pi, None, ALU.max))
            pool.tensor_scalar(cos_arg[:, :], ang[:, :], 0.0, None, ALU.max)
            chain(pool.tensor_scalar(turns[:, :], ang[:, :], 0.0, None, ALU.min))
            chain(pool.tensor_tensor(cos_arg[:, :], cos_arg[:, :], turns[:, :], ALU.subtract))
            pool.tensor_scalar(cos_arg[:, :], cos_arg[:, :], -1.0, np.pi / 2, ALU.mult, ALU.add) \
                .then_inc(trig_args, 1)
            pool.wait_ge(trig_ready, 1)

            def rotate(which):
                v = qk_tok[:, which, :, :].rearrange("p h (n d) -> p h n d", n=HEADS)
                x1, x2 = v[:, :, :, 0:RHALF], v[:, :, :, RHALF:ROPE]
                shape = [P, HALVES, HEADS, RHALF]
                cos, sin = (t[:, :, :].unsqueeze(2).to_broadcast(shape) for t in (cos_t, sin_t))
                r = [rot[:, n, :, :].rearrange("p h (n d) -> p h n d", n=HEADS) for n in range(4)]
                pool.tensor_tensor(r[0], x1, cos, ALU.mult)
                pool.tensor_tensor(r[1], x2, sin, ALU.mult)
                pool.tensor_tensor(r[2], x2, cos, ALU.mult)
                chain(pool.tensor_tensor(r[3], x1, sin, ALU.mult))
                pool.tensor_tensor(x1, r[0], r[1], ALU.subtract)
                pool.tensor_tensor(x2, r[2], r[3], ALU.add).then_inc(rotated, 1)

            steps = 2
            start = chain.n
            with pool.Fori(0, GROUPS) as i:
                chain.at(start + steps * i)
                for h in range(HEADS):
                    pool.wait_ge(sp_ready, HEADS * i + h + 1)
                    pool.tensor_tensor(s_a[:, h % 2, 0:2 * P], s_a[:, h % 2, 0:2 * P],
                                       past_one[:, :], ALU.mult).then_inc(sp_masked, 1)
                    if h in (1, 3):
                        pool.wait_ge(evac, 7 * i + 4 + h // 2)
                        rotate(h // 2)
                assert chain.n == steps

        @block.scalar
        def _(act):
            chain = Chain(act, act_step)

            def hi(n, s):
                act.wait_ge(raw_landed[s], 4 * n + (16 - 4 * s))
                act.wait_ge(piece_used, n + 1)
                act.copy(w_hi[:, s, :], w_raw[:, s, :]).then_inc(hi_ready, 1)

            def turned_hi(t, dst, tile0, gain0, banks):
                act.wait_ge(t_done, t + 1)
                for b in range(2):
                    for kk in (2 * b, 2 * b + 1):
                        ins = act.activation(dst[:, tile0 + kk, :],
                                             banks[:, b, (kk % 2) * S:(kk % 2 + 1) * S], ACT.Copy,
                                             scale=g_col[:, gain0 + kk:gain0 + kk + 1])
                    ins.then_inc(t_hi_ready, 1)

            def evacuate(n_end, banks, dst, rstd):
                act.wait_ge(piece_used, n_end + SLOTS)
                for hf in range(HALVES):
                    ins = act.activation(dst[:, hf, :], banks[:, hf, :], ACT.Copy,
                                         scale=rstd[:, hf:hf + 1])
                ins.then_inc(evac, 1)

            def inverse_root(norm, cols):
                act.wait_ge(ms_ready, norm + 1)
                chain(act.activation(ln_ms[:, 0:cols], ms[:, 0:cols], ACT.Ln))
                act.activation(rs[:, 0:cols], ln_ms[:, 0:cols], ACT.Exp, scale=-0.5) \
                    .then_inc(root_ready, 1)

            def square_heads(group):
                act.wait_ge(heads_done, group + 1)
                for hf in range(HALVES):
                    ins = act.activation(s_a[:, hf, :], pair(3)[:, hf, :], ACT.Square)
                ins.then_inc(ssq_ready, 1)

            def exponentials(n, h, last, scales=None):
                act.wait_ge(max_ready, n + 1)
                b = h % 2
                for hf, cols in ((0, slice(0, last)), (1, slice(last, 512 if last == S else 3 * P))):
                    ins = act.activation(s_b[:, b, cols], s_a[:, b, cols], ACT.Exp,
                                         bias=negmax[:, b, hf:hf + 1],
                                         scale=SCALE if scales is None else scales[:, hf:hf + 1],
                                         accum_out=rowsum[:, hf * HEADS + h:hf * HEADS + h + 1])
                ins.then_inc(p_ready, 1)

            def square_input(norm, src, part):
                hf, q = part // 2, part % 2
                at = 4 * norm + part
                chain(act.activation(wide, src[:, hf, q * PIECE:(q + 1) * PIECE], ACT.Square,
                                     accum_out=ssq[:, at:at + 1]))
                if part == 3:
                    act.sem_inc(ssq_ready, 1)

            rows = [(g_mix, G_MIX), (g_mem, G_MEM), (g_xattn, G_X), (g_ffn, G_FFN),
                    (g_out_sb, G_O), (g_out_moba, G_O + W_SB // P)]
            for g, at in rows:
                n = g.shape[0] // P
                act.dma_start(g_rows[at:at + n, :], g.rearrange("(t p) -> t p", p=P)) \
                    .then_inc(gains_landed, 16)
            act.dma_start(pos_i[:, :], positions[0, :].rearrange("(h p) -> p h", p=P),
                          allow_slow_non_contiguous=True) \
                .then_inc(pos_landed, 16)
            act.wait_ge(gains_ready, 1)
            turned_hi(0, t0_hi, 0, G_MIX, pair(2))
            for c in range(TG):
                cols = slice(c * W_GROUP, (c + 1) * W_GROUP)
                act.dma_start(o_tok[:, :, cols], mem[0, :, cols].rearrange("(h p) c -> p h c", p=P)) \
                    .then_inc(mem_landed[c], 16)
            turned_hi(1, t0_hi, 4, G_MIX + 4, pair(3))
            hi(0, 0)
            turned_hi(2, t0_hi, 8, G_MIX + 8, pair(2))
            turned_hi(3, t0_hi, 12, G_MIX + 12, pair(3))
            hi(1, 1)
            act.preload_act_table_set("natural_log_exp_and_others")

            for i in range(GROUPS):
                n0 = MIX_STEP * i
                for s in range(MIX_STEP):
                    hi(n0 + s + LEAD, (s + LEAD) % SLOTS)
                    if i == 0:
                        if s in (0, 2, 4, 5):
                            square_input(NORM_X, x_tok, (0, 2, 4, 5).index(s))
                        if s in (1, 3, 5, 7):
                            c = s // 2
                            turned_hi(T_MEM + c, t1_hi, 4 * c, G_MEM + 4 * c, pair(2 + c % 2))
                        if s == 6:
                            inverse_root(NORM_X, HALVES)
                            act.wait_ge(rstd_ready, 1)
                        if 9 <= s < 13:
                            square_input(NORM_MEM, o_tok, s - 9)
                        if s == 14:
                            inverse_root(NORM_MEM, HALVES)
                            act.wait_ge(rstd_ready, 2)
                        if s == 16:
                            act.wait_ge(trig_args, 1)
                            act.activation(sin_t[:, :, :].rearrange("p h f -> p (h f)"), ang[:, :],
                                           ACT.Sin)
                            act.activation(cos_t[:, :, :].rearrange("p h f -> p (h f)"),
                                           cos_arg[:, :], ACT.Sin).then_inc(trig_ready, 1)
                            act.preload_act_table_set("natural_log_exp_and_others")
                    if s % CP == CP - 1:
                        c = s // CP
                        dst = [qk_tok[:, 0], qk_tok[:, 1], v_tok[:, 0], qk_tok[:, 0],
                               qk_tok[:, 1], v_tok[:, 1], kvx_tok[:, i]][c]
                        evacuate(n0 + s + 1, pair(c % 2), dst, rstd_m if c == 6 else rstd_x)
                    for h in range(HEADS):
                        if s == 3 * CP + 4 * h:
                            b = h % 2
                            act.wait_ge(z_done, HEADS * i + h + 1)
                            chain(act.activation(s_b[:, b, 0:384], pair(2)[:, b, 0:384], ACT.Abs))
                            chain(act.activation(s_b[:, b, 0:384], s_b[:, b, 0:384], ACT.Exp,
                                                 scale=-1.0))
                            act.activation(s_b[:, b, 0:384], s_b[:, b, 0:384], ACT.Ln, bias=1.0) \
                                .then_inc(log_ready, 1)
                        if s == 3 * CP + 4 * h + 3:
                            act.wait_ge(cum_done, HEADS * i + h + 1)
                            act.activation(s_c[:, h % 2, 0:384], pair(2)[:, h % 2, 0:384], ACT.Exp) \
                                .then_inc(w_exp, 1)
                        if s == 46 + 2 * h:
                            exponentials(HEADS * i + h, h, P)
                    if s == 42:
                        square_heads(2 * i)
                    if s == 43:
                        inverse_root(NORM_HEADS + 2 * i, 8)
                    if i == GROUPS - 1 and s in (50, 53):
                        c = (s - 50) // 3
                        turned_hi(T_O + c, t0_hi, 4 * c, G_O + 4 * c, pair(1))
                    if s == 55:
                        square_heads(2 * i + 1)
                        inverse_root(NORM_HEADS + 2 * i + 1, 8)

            def square_chunk(first, c):
                act.wait_ge(resid, first + c + 1)
                for hf in range(HALVES):
                    at = hf * TG + c
                    chain(act.activation(wide[:, 0:W_GROUP],
                                         x_tok[:, hf, c * W_GROUP:(c + 1) * W_GROUP],
                                         ACT.Square, accum_out=ssq[:, at:at + 1]))
                if c == TG - 1:
                    act.sem_inc(ssq_ready, 1)

            for s in range(TG * CP):
                n = P_WOUT + s + LEAD
                hi(n, n % SLOTS)
                if s in (0, 3):
                    c = 2 + s // 3
                    turned_hi(T_O + c, t0_hi, 4 * c, G_O + 4 * c, pair(2))
                if s % CP == CP - 1:
                    square_chunk(0, s // CP)
                if s >= CP and s % CP == 2:
                    c = s // CP - 1
                    turned_hi(T_WOUT + c, t1_hi, 4 * c, G_X + 4 * c, pair(2))

            def q_copy(h, e):
                act.wait_ge(piece_used, P_XQ + e + 1 + SLOTS)
                act.copy(qT[:, 0, h, :], pair(1)[:, h % 2, 0:S]).then_inc(evac, 1)

            def head_hi(h):
                act.wait_ge(heads_done, 2 * GROUPS + h + 1)
                act.copy(t0_hi[:, h, :], pair(3)[:, h % 2, 0:S]).then_inc(o_hi_ready, 1)

            cross = GROUPS * HEADS
            for s in range(CP):
                n = P_XQ + s + LEAD
                hi(n, n % SLOTS)
                if s == 0:
                    turned_hi(T_WOUT + TG - 1, t1_hi, KT - 4, G_X + KT - 4, pair(2))
                if s == 1:
                    inverse_root(NORM_Q, HALVES)
                    act.wait_ge(rstd_ready, 3)
                if s == 2:
                    q_copy(0, 2)
                if s == 3:
                    q_copy(1, 3)
                    exponentials(cross, 0, S, scale_q)
                if s == 4:
                    exponentials(cross + 1, 1, S, scale_q)
                if s == 5:
                    q_copy(2, 5)
                if s == 6:
                    head_hi(0)
                    exponentials(cross + 2, 2, S, scale_q)
                if s == 7:
                    q_copy(3, 7)
                    head_hi(1)
                    exponentials(cross + 3, 3, S, scale_q)
                    head_hi(2)
            for s in range(TG * XP):
                n = P_XO + s + LEAD
                hi(n, n % SLOTS)
                if s == 1:
                    head_hi(3)
                if XO_PIECES[s][1] == 1:
                    square_chunk(TG, XO_PIECES[s][0])
                if s in (4, 5, 7):
                    c = (4, 5, 7).index(s)
                    turned_hi(T_XO + c, t1_hi, 4 * c, G_FFN + 4 * c, pair(2))
            for s in range(CP):
                n = P_GATE0 + s + LEAD
                hi(n, n % SLOTS)
                if s == 1:
                    turned_hi(T_XO + TG - 1, t1_hi, KT - 4, G_FFN + KT - 4, pair(2))
                    inverse_root(NORM_F, HALVES)
            act.wait_ge(rstd_ready, 4)
            act.preload_act_table_set("silu_and_others")

            def silu(i, n_end):
                act.wait_ge(piece_used, n_end + SLOTS)
                act.wait_ge(h_ready, i + 1)
                for hf in range(HALVES):
                    ins = act.activation(qk_tok[:, 0, hf, :], pair(0)[:, hf, :], ACT.Silu,
                                         scale=rstd_f[:, hf:hf + 1])
                ins.then_inc(silu_out, 1)

            with act.Fori(0, FC - 1) as i:
                for s in range(2 * CP):
                    n = P_FFN + 2 * CP * i + s
                    hi(n + LEAD, (s + LEAD) % SLOTS)
                    if s == 0:
                        silu(i, n)
            for s in range(CP):
                n = P_FFN + 2 * CP * (FC - 1) + s
                hi(n + LEAD, (s + LEAD) % SLOTS)
                if s == 0:
                    silu(FC - 1, n)

            def h_upper(k, s):
                act.wait_ge(piece_used, 2 * k + (P_DOWN + SLOTS - 2 * SLOTS + 2))
                act.copy(h_hi[:, s, :], hT[:, bass.ds(k, 1), :].rearrange("p k t -> p (k t)")) \
                    .then_inc(h_hi_ready, 1)

            def down(i, last=False):
                for kk in range(SLOTS):
                    if not (last and kk == SLOTS - 1):
                        h_upper(SLOTS * i + kk + 1, (kk + 1) % SLOTS)
                        for j in (0, 1):
                            hi(P_DOWN + LEAD + DOWN_STEP * i + 2 * kk + j, (2 * kk + j + LEAD) % SLOTS)

            act.wait_ge(t_out, T_END - 1)
            act.dma_start(gfin[:, :], g_final.partition_broadcast(P)).then_inc(gfin_landed, 16)
            h_upper(0, 0)
            act.preload_act_table_set("natural_log_exp_and_others")
            with act.Fori(0, FK // SLOTS - 1) as i:
                down(i)
            down(FK // SLOTS - 1, last=True)
            for hf in range(HALVES):
                for c in range(TG):
                    act.wait_ge(resid, 2 * TG + hf * TG + c + 1)
                    ins = act.activation(wide[:, 0:W_GROUP],
                                         x_tok[:, hf, c * W_GROUP:(c + 1) * W_GROUP],
                                         ACT.Square, accum_out=ssq[:, hf * TG + c:hf * TG + c + 1])
                    chain(ins)
                act.sem_inc(ssq_ready, 1)
                inverse_root(NORM_OUT + hf, 1)

        @block.vector
        def _(dve):
            chain = Chain(dve, dve_step)

            def lo(n, s):
                dve.wait_ge(hi_ready, n + 1)
                dve.tensor_tensor(w_lo[:, s, :], w_raw[:, s, :], w_hi[:, s, :].bitcast(F32),
                                  ALU.subtract).then_inc(lo_ready, 1)

            def turned_lo(group, dst, dst_hi, tile0, gain0, banks):
                for b in range(2):
                    dve.wait_ge(t_hi_ready, 2 * group + b + 1)
                    for kk in (2 * b, 2 * b + 1):
                        ins = dve.scalar_tensor_tensor(
                            out=dst[:, tile0 + kk, :],
                            in0=banks[:, b, (kk % 2) * S:(kk % 2 + 1) * S],
                            scalar=g_col[:, gain0 + kk:gain0 + kk + 1],
                            in1=dst_hi[:, tile0 + kk, :].bitcast(F32),
                            op0=ALU.mult, op1=ALU.subtract)
                ins.then_inc(t_out, 1)

            def turned_out(t, dst, scale):
                dve.wait_ge(t_done, t + 1)
                for b in range(2):
                    ins = dve.tensor_scalar(
                        dst[:, 2 * b:2 * b + 2, :].rearrange("p n t -> p (n t)"),
                        pair(2)[:, b, :], scale, None, ALU.mult)
                ins.then_inc(t_out, 1)

            def refine(norm, cols, dst):
                dve.wait_ge(root_ready, norm + 1)
                y, m, t = rs[:, 0:cols], ms[:, 0:cols], nt[:, 0:cols]
                chain(dve.tensor_tensor(t, y, y, ALU.mult))
                chain(dve.tensor_tensor(t, t, m, ALU.mult))
                chain(dve.tensor_scalar(t, t, -0.5, 1.5, ALU.mult, ALU.add))
                return dve.tensor_tensor(dst, y, t, ALU.mult)

            def head_squares(norm, softmax):
                if softmax:
                    chain(dve.reciprocal(rden[:, 0:8], rowsum[:, :]))
                    dve.tensor_tensor(fac[:, 0:8], rden[:, 0:8], rden[:, 0:8], ALU.mult)
                dve.wait_ge(ssq_ready, norm + 1)
                for hf in range(HALVES):
                    ins = dve.tensor_reduce(ssq[:, hf * HEADS:(hf + 1) * HEADS],
                                            s_a[:, hf, :].rearrange("p (n d) -> p n d", n=HEADS),
                                            AX.X, ALU.add)
                chain(ins)
                if softmax:
                    chain(dve.tensor_tensor(ssq[:, 0:8], ssq[:, 0:8], fac[:, 0:8], ALU.mult))
                dve.tensor_scalar(ms[:, 0:8], ssq[:, 0:8], 1.0 / HD, EPS, ALU.mult, ALU.add) \
                    .then_inc(ms_ready, 1)

            def head_outputs(norm, softmax, col):
                chain(refine(norm, 8, fac[:, 0:8]))
                if softmax:
                    chain(dve.tensor_tensor(fac[:, 0:8], fac[:, 0:8], rden[:, 0:8], ALU.mult))
                scale_heads(o_tok, col)

            def scale_heads(dst, col):
                for hf in range(HALVES):
                    f = fac[:, hf * HEADS:(hf + 1) * HEADS].unsqueeze(2).to_broadcast([P, HEADS, HD])
                    ins = dve.tensor_tensor(
                        dst[:, hf, bass.ds(col, W_GROUP)].rearrange("p (n d) -> p n d", n=HEADS),
                        pair(3)[:, hf, :].rearrange("p (n d) -> p n d", n=HEADS), f, ALU.mult)
                ins.then_inc(o_out, 1)

            def scores_out(n, h, mask):
                b = h % 2
                dve.wait_ge(s_done, n + 1)
                width = 3 * P if mask else 2 * S
                last = P if mask else S
                if mask:
                    ins = dve.tensor_tensor(s_a[:, b, 0:width], pair(2)[:, 0, 0:width],
                                            causal[:, :], ALU.add)
                else:
                    ins = dve.tensor_copy(s_a[:, b, 0:width], pair(2)[:, 0, 0:width])
                ins.then_inc(s_out, 1)
                dve.wait_ge(s_out, n + 1)
                dve.tensor_reduce(negmax[:, b, 0:1], s_a[:, b, 0:last], AX.X, ALU.max)
                chain(dve.tensor_reduce(negmax[:, b, 1:2], s_a[:, b, last:width], AX.X, ALU.max))
                if mask:
                    ins = dve.tensor_scalar(negmax[:, b, :], negmax[:, b, :], -SCALE, None, ALU.mult)
                else:
                    ins = dve.scalar_tensor_tensor(out=negmax[:, b, :], in0=negmax[:, b, :],
                                                   scalar=-1.0, in1=scale_q[:, :],
                                                   op0=ALU.mult, op1=ALU.mult)
                ins.then_inc(max_ready, 1)

            def probs_out(n, h, width):
                dve.wait_ge(pt_done, n + 1)
                dve.tensor_copy(s_c[:, h % 2, 0:width], pair(2)[:, 1, 0:width]).then_inc(pt_out, 1)

            def row_ms(norm, cols, cuts, first=0):
                dve.wait_ge(ssq_ready, norm + 1)
                part = ssq[:, first:first + cols * cuts]
                chain(dve.tensor_reduce(nt[:, 0:cols], part.rearrange("p (n c) -> p n c", c=cuts),
                                        AX.X, ALU.add))
                dve.tensor_scalar(ms[:, 0:cols], nt[:, 0:cols], 1.0 / D, EPS, ALU.mult, ALU.add) \
                    .then_inc(ms_ready, 1)

            dve.sem_inc(lo_ready, SLOTS)
            dve.sem_inc(h_ready, 1)

            dve.wait_ge(gains_turned, 1)
            dve.tensor_copy(g_col[:, :], psum[:, 0, 0:G_ROWS]).then_inc(gains_ready, 1)
            dve.wait_ge(gains_ready, 1)
            for c in range(TG):
                turned_lo(c, t0_lo, t0_hi, 4 * c, G_MIX + 4 * c, pair(2 + c % 2))
                if c in (1, 3):
                    lo(c // 2, c // 2)

            for i in range(GROUPS):
                n0 = MIX_STEP * i
                t0 = 4 * i + T_MIX
                for s in range(MIX_STEP):
                    lo(n0 + s + LEAD, (s + LEAD) % SLOTS)
                    if i == 0:
                        if s in (1, 3, 5, 7):
                            c = s // 2
                            turned_lo(SPLIT_MEM + c, t1_lo, t1_hi, 4 * c, G_MEM + 4 * c,
                                      pair(2 + c % 2))
                        if s == 6:
                            row_ms(NORM_X, HALVES, 2)
                            refine(NORM_X, HALVES, rstd_x[:, :]).then_inc(rstd_ready, 1)
                        if s == 14:
                            row_ms(NORM_MEM, HALVES, 2, first=4)
                            refine(NORM_MEM, HALVES, rstd_m[:, :]).then_inc(rstd_ready, 1)
                    if s == CP + 2:
                        turned_out(t0, qT[:, 0], SCALE)
                    if s == 2 * CP + 2:
                        turned_out(t0 + 1, kT[:, 0], 1.0)
                    for h in range(HEADS):
                        if s == 3 * CP + 4 * h + 1:
                            b = h % 2
                            dve.wait_ge(log_ready, HEADS * i + h + 1)
                            dve.scalar_tensor_tensor(out=s_a[:, b, 0:384],
                                                     in0=pair(2)[:, b, 0:384], scalar=0.0,
                                                     in1=s_b[:, b, 0:384], op0=ALU.max,
                                                     op1=ALU.add).then_inc(sp_ready, 1)
                        if s == 46 + 2 * h:
                            scores_out(HEADS * i + h, h, True)
                        if s == 48 + 2 * h:
                            probs_out(HEADS * i + h, h, 3 * P)
                    if s == 42:
                        turned_out(t0 + 2, qT[:, 1], 1.0)
                    if s == 43:
                        head_squares(NORM_HEADS + 2 * i, False)
                    if s == 44:
                        head_outputs(NORM_HEADS + 2 * i, False, W_GROUP * i)
                        turned_out(t0 + 3, kT[:, 1], 1.0)
                    if i == GROUPS - 1 and s in (50, 53):
                        c = (s - 50) // 3
                        turned_lo(SPLIT_O + c, t0_lo, t0_hi, 4 * c, G_O + 4 * c, pair(1))
                    if s == 55:
                        head_squares(NORM_HEADS + 2 * i + 1, True)
                        head_outputs(NORM_HEADS + 2 * i + 1, True, W_SB + W_GROUP * i)

            def add_residual(n_end, banks, c):
                dve.wait_ge(piece_used, n_end + SLOTS)
                for hf in range(HALVES):
                    x_part = x_tok[:, hf, c * W_GROUP:(c + 1) * W_GROUP]
                    ins = dve.tensor_tensor(x_part, banks[:, hf, :], x_part, ALU.add)
                ins.then_inc(resid, 1)

            for s in range(TG * CP):
                n = P_WOUT + s + LEAD
                lo(n, n % SLOTS)
                if s in (0, 3):
                    c = 2 + s // 3
                    turned_lo(SPLIT_O + c, t0_lo, t0_hi, 4 * c, G_O + 4 * c, pair(2))
                if s == 6:
                    turned_out(T_KX, kT[:, 0], 1.0)
                if s % CP == CP - 1:
                    add_residual(P_WOUT + s + 1, pair((s // CP + 1) % 2), s // CP)
                if s >= CP and s % CP == 2:
                    c = s // CP - 1
                    turned_lo(SPLIT_WOUT + c, t1_lo, t1_hi, 4 * c, G_X + 4 * c, pair(2))

            def diagonals(h):
                dve.wait_ge(p_ready, cross + h + 1)
                inv = rden[:, 2 * (h % 2):2 * (h % 2) + 2]
                sums = rowsum[:, :].rearrange("p (a b) -> p a b", b=HEADS)[:, :, h]
                chain(dve.reciprocal(inv, sums))
                for hf in range(HALVES):
                    ins = dve.tensor_scalar(qk_tok[:, 0, h % 2, hf * P:(hf + 1) * P], ident[:, :],
                                            inv[:, hf:hf + 1], None, ALU.mult)
                ins.then_inc(diag_ready, 1)

            def head_lo(h):
                dve.wait_ge(o_hi_ready, h + 1)
                dve.tensor_tensor(t0_lo[:, h, :], pair(3)[:, h % 2, 0:S],
                                  t0_hi[:, h, :].bitcast(F32), ALU.subtract).then_inc(o_out, 1)

            cross = GROUPS * HEADS
            for s in range(CP):
                n = P_XQ + s + LEAD
                lo(n, n % SLOTS)
                if s == 0:
                    turned_lo(SPLIT_WOUT + TG - 1, t1_lo, t1_hi, KT - 4, G_X + KT - 4, pair(2))
                if s == 1:
                    row_ms(NORM_Q, HALVES, TG)
                    chain(refine(NORM_Q, HALVES, fac[:, 0:HALVES]))
                    dve.tensor_scalar(scale_q[:, :], fac[:, 0:HALVES], SCALE, None, ALU.mult) \
                        .then_inc(rstd_ready, 1)
                    dve.wait_ge(rstd_ready, 3)
                if s == 3:
                    scores_out(cross, 0, False)
                if s == 4:
                    diagonals(0)
                    scores_out(cross + 1, 1, False)
                if s == 5:
                    probs_out(cross, 0, 2 * S)
                    diagonals(1)
                if s == 6:
                    probs_out(cross + 1, 1, 2 * S)
                    scores_out(cross + 2, 2, False)
                    head_lo(0)
                if s == 7:
                    diagonals(2)
                    head_lo(1)
                    probs_out(cross + 2, 2, 2 * S)
                    scores_out(cross + 3, 3, False)
            for s in range(TG * XP):
                n = P_XO + s + LEAD
                lo(n, n % SLOTS)
                if s == 0:
                    diagonals(3)
                    head_lo(2)
                if s == 1:
                    probs_out(cross + 3, 3, 2 * S)
                    head_lo(3)
                if XO_PIECES[s][1] == 1:
                    c = XO_PIECES[s][0]
                    add_residual(P_XO + s + 1, pair(c % 2), c)
                if s in (4, 5, 7):
                    c = (4, 5, 7).index(s)
                    turned_lo(SPLIT_XO + c, t1_lo, t1_hi, 4 * c, G_FFN + 4 * c, pair(2))
            for s in range(CP):
                n = P_GATE0 + s + LEAD
                lo(n, n % SLOTS)
                if s == 1:
                    turned_lo(SPLIT_XO + TG - 1, t1_lo, t1_hi, KT - 4, G_FFN + KT - 4, pair(2))
                    row_ms(NORM_F, HALVES, TG)
                    refine(NORM_F, HALVES, rstd_f[:, :]).then_inc(rstd_ready, 1)
            dve.wait_ge(rstd_ready, 4)

            def hidden(i, n_end):
                dve.wait_ge(piece_used, n_end + SLOTS)
                dve.wait_ge(silu_out, i + 1)
                for hf in range(HALVES):
                    ins = dve.scalar_tensor_tensor(out=qk_tok[:, 1, hf, :], in0=pair(1)[:, hf, :],
                                                   scalar=rstd_f[:, hf:hf + 1],
                                                   in1=qk_tok[:, 0, hf, :],
                                                   op0=ALU.mult, op1=ALU.mult)
                ins.then_inc(h_ready, 1)

            def hidden_turned(i):
                dve.wait_ge(t_done, i + (T_H + 1))
                for b in range(2):
                    ins = dve.tensor_copy(
                        hT[:, bass.ds(4 * i + 2 * b, 2), :].rearrange("p k t -> p (k t)"),
                        pair(2)[:, b, :])
                ins.then_inc(t_out, 1)

            with dve.Fori(0, FC - 1) as i:
                for s in range(2 * CP):
                    n = P_FFN + 2 * CP * i + s
                    lo(n + LEAD, (s + LEAD) % SLOTS)
                    if s == CP - 1:
                        hidden(i, n + 1)
                    if s == CP + 2:
                        hidden_turned(i)
            for s in range(CP):
                n = P_FFN + 2 * CP * (FC - 1) + s
                lo(n + LEAD, (s + LEAD) % SLOTS)
            hidden(FC - 1, P_DOWN)

            def h_rest(k, s):
                dve.wait_ge(h_hi_ready, k + 1)
                dve.tensor_tensor(h_lo[:, s, :], hT[:, bass.ds(k, 1), :].rearrange("p k t -> p (k t)"),
                                  h_hi[:, s, :].bitcast(F32), ALU.subtract).then_inc(h_split, 1)

            def down(i, last=False):
                for kk in range(SLOTS):
                    if not (last and kk == SLOTS - 1):
                        h_rest(SLOTS * i + kk + 1, (kk + 1) % SLOTS)
                        for j in (0, 1):
                            lo(P_DOWN + LEAD + DOWN_STEP * i + 2 * kk + j, (2 * kk + j + LEAD) % SLOTS)

            h_rest(0, 0)
            hidden_turned(FC - 1)
            with dve.Fori(0, FK // SLOTS - 1) as i:
                down(i)
            down(FK // SLOTS - 1, last=True)

            dve.wait_ge(gfin_landed, 16)
            for hf in range(HALVES):
                for c in range(TG):
                    x_part = x_tok[:, hf, c * W_GROUP:(c + 1) * W_GROUP]
                    dve.wait_ge(bank_done, hf * TG + c + 1)
                    dve.tensor_tensor(x_part, down_bank(hf, c), x_part, ALU.add) \
                        .then_inc(resid, 1)
                norm = NORM_OUT + hf
                dve.wait_ge(ssq_ready, norm + 1)
                chain(dve.tensor_reduce(nt[:, 0:1], ssq[:, hf * TG:(hf + 1) * TG], AX.X, ALU.add))
                dve.tensor_scalar(ms[:, 0:1], nt[:, 0:1], 1.0 / D, EPS, ALU.mult, ALU.add) \
                    .then_inc(ms_ready, 1)
                chain(refine(norm, 1, rstd_o[:, hf:hf + 1]))
                for q in range(2):
                    cols = slice(q * PIECE, (q + 1) * PIECE)
                    dve.scalar_tensor_tensor(out=x_tok[:, hf, cols], in0=x_tok[:, hf, cols],
                                             scalar=rstd_o[:, hf:hf + 1], in1=gfin[:, cols],
                                             op0=ALU.mult, op1=ALU.mult).then_inc(final_ready, 1)

        @block.tensor
        def _(pe):
            def product(n, banks, t_hi, t_lo, ready=None, hook=None):
                pieces = CP
                for j in range(pieces):
                    s = j % SLOTS
                    if ready is not None and j % 2 == 0:
                        pe.wait_ge(t_out, ready + j // 2 + 1)
                    pe.wait_ge(lo_ready, n + (j + 1 + SLOTS))
                    for kk in range(2):
                        k = 2 * j + kk
                        wh = w_hi[:, s, kk * W_GROUP:(kk + 1) * W_GROUP]
                        wl = w_lo[:, s, kk * W_GROUP:(kk + 1) * W_GROUP]
                        for hf in range(HALVES):
                            th = t_hi[:, k, hf * P:(hf + 1) * P]
                            tl = t_lo[:, k, hf * P:(hf + 1) * P]
                            first, last = k == 0, k == 2 * pieces - 1
                            pe.matmul(banks[:, hf, :], lhsT=th, rhs=wh, start=first, stop=False)
                            pe.matmul(banks[:, hf, :], lhsT=th, rhs=wl, start=False, stop=False)
                            mm = pe.matmul(banks[:, hf, :], lhsT=tl, rhs=wh, start=False, stop=last)
                    mm.then_inc(piece_used, 1)
                    if hook:
                        hook(j)

            def turn(banks, src, n_blocks=4):
                for kk in range(n_blocks):
                    for hf in range(HALVES):
                        at = (kk % 2) * S + hf * P
                        mm = pe.transpose(banks[:, kk // 2, at:at + P],
                                          src[:, hf, kk * P:(kk + 1) * P], ident[:, :])
                mm.then_inc(t_done, 1)

            pe.sem_inc(piece_used, SLOTS)
            pe.wait_ge(consts_ready, 1)
            for c in range(TG):
                pe.wait_ge(x_landed[c], 16)
                if c >= 2:
                    pe.wait_ge(t_out, c - 1)
                turn(pair(2 + c % 2), x_tok[:, :, c * W_GROUP:(c + 1) * W_GROUP])
                if c == 1:
                    pe.wait_ge(gains_landed, 16 * 6)
                    pe.transpose(psum[:, 0, 0:G_ROWS], g_rows[:, :], ident[0:G_ROWS, 0:G_ROWS]) \
                        .then_inc(gains_turned, 1)

            def z_scores(n, h):
                z = pair(2)[:, h % 2, :]
                k0, k1 = kT[:, 0, h, 0:P], kT[:, 0, h, P:S]
                q0, q1 = qT[:, 0, h, 0:P], qT[:, 0, h, P:S]
                pe.matmul(z[:, 0:P], lhsT=k0, rhs=q0, start=True, stop=True, skip_group_check=True)
                pe.matmul(z[:, P:2 * P], lhsT=k1, rhs=q1, start=False, stop=True,
                          skip_group_check=True)
                pe.matmul(z[:, 2 * P:3 * P], lhsT=k0, rhs=q1, start=False, stop=True,
                          skip_group_check=True).then_inc(z_done, 1)

            def reverse_sums(n, h):
                pe.wait_ge(sp_masked, n + 1)
                z, sp = pair(2)[:, h % 2, :], s_a[:, h % 2, :]
                pe.matmul(z[:, 0:2 * P], lhsT=ident_r[:, :], rhs=not_past[:, :], start=False,
                          stop=True, skip_group_check=True)
                pe.matmul(z[:, 0:3 * P], lhsT=neg_tri[:, :], rhs=sp[:, 0:3 * P], start=False,
                          stop=True, skip_group_check=True)
                pe.matmul(z[:, 2 * P:3 * P], lhsT=neg_one[:, :], rhs=sp[:, P:2 * P], start=False,
                          stop=True, skip_group_check=True).then_inc(cum_done, 1)

            def values(h, v):
                w, cols = s_c[:, h % 2, :], slice(h * HD, (h + 1) * HD)
                o = pair(3)
                pe.matmul(o[:, 0, cols], lhsT=w[:, 0:P], rhs=v[:, 0, cols], start=True, stop=True)
                pe.matmul(o[:, 1, cols], lhsT=w[:, 2 * P:3 * P], rhs=v[:, 0, cols], start=True,
                          stop=False)
                mm = pe.matmul(o[:, 1, cols], lhsT=w[:, P:2 * P], rhs=v[:, 1, cols], start=False,
                               stop=True)
                if h == HEADS - 1:
                    mm.then_inc(heads_done, 1)

            def scores(h):
                sc = pair(2)[:, 0, :]
                q0, q1 = qT[:, 1, h, 0:P], qT[:, 1, h, P:S]
                k0, k1 = kT[:, 1, h, 0:P], kT[:, 1, h, P:S]
                pe.matmul(sc[:, 0:P], lhsT=q0, rhs=k0, start=True, stop=True)
                pe.matmul(sc[:, P:2 * P], lhsT=q1, rhs=k1, start=True, stop=True)
                pe.matmul(sc[:, 2 * P:3 * P], lhsT=q1, rhs=k0, start=True, stop=True) \
                    .then_inc(s_done, 1)

            def turn_probs(n, h, blocks):
                pe.wait_ge(p_ready, n + 1)
                for b, src in enumerate(blocks):
                    mm = pe.transpose(pair(2)[:, 1, b * P:(b + 1) * P],
                                      s_b[:, h % 2, src * P:(src + 1) * P], ident[:, :])
                mm.then_inc(pt_done, 1)

            def mixer_hook(i, s):
                t0 = 4 * i + T_MIX
                if i == 0 and s in (1, 3, 5, 7):
                    c = s // 2
                    pe.wait_ge(mem_landed[c], 16)
                    pe.wait_ge(t_out, T_MEM + c - 1)
                    turn(pair(2 + c % 2), o_tok[:, :, c * W_GROUP:(c + 1) * W_GROUP])
                if s == CP + 2:
                    pe.wait_ge(evac, 7 * i + 1)
                    pe.wait_ge(t_out, t0)
                    turn(pair(2), qk_tok[:, 0])
                if s == 2 * CP + 2:
                    pe.wait_ge(evac, 7 * i + 2)
                    pe.wait_ge(t_out, t0 + 1)
                    turn(pair(2), qk_tok[:, 1])
                for h in range(HEADS):
                    n = HEADS * i + h
                    if s == 3 * CP + 4 * h:
                        if h == 0:
                            pe.wait_ge(t_out, t0 + 2)
                            pe.wait_ge(evac, 7 * i + 3)
                        if h >= 2:
                            pe.wait_ge(w_exp, n - 1)
                        z_scores(n, h)
                    if s == 3 * CP + 4 * h + 2:
                        reverse_sums(n, h)
                    if s == 3 * CP + 4 * h + 5:
                        if h == 0 and i:
                            pe.wait_ge(o_out, 2 * i)
                        pe.wait_ge(w_exp, n + 1)
                        values(h, v_tok[:, 0])
                    if s == 46 + 2 * h:
                        if h == 0:
                            pe.wait_ge(t_out, t0 + 4)
                        else:
                            pe.wait_ge(s_out, n)
                        scores(h)
                    if s == 48 + 2 * h:
                        if h >= 1:
                            pe.wait_ge(pt_out, n)
                        turn_probs(n, h, (0, 1, 2))
                    if s == min(50 + 2 * h, 55):
                        if h == 0:
                            pe.wait_ge(o_out, 2 * i + 1)
                            pe.wait_ge(evac, 7 * i + 6)
                        pe.wait_ge(pt_out, n + 1)
                        values(h, v_tok[:, 1])
                if s == 42:
                    pe.wait_ge(rotated, 2 * i + 1)
                    pe.wait_ge(w_exp, HEADS * i + HEADS)
                    turn(pair(2), qk_tok[:, 0])
                if s == 44:
                    pe.wait_ge(rotated, 2 * i + 2)
                    pe.wait_ge(t_out, t0 + 3)
                    turn(pair(2), qk_tok[:, 1])
                if i == GROUPS - 1 and s in (50, 53):
                    c = (s - 50) // 3
                    pe.wait_ge(t_out, T_O + c)
                    if c == 1:
                        pe.wait_ge(o_out, 2 * i + 1)
                    turn(pair(1), o_tok[:, :, c * W_GROUP:(c + 1) * W_GROUP])

            for i in range(GROUPS):
                for c in range(7):
                    if c >= 2:
                        pe.wait_ge(evac, 7 * i + c - 1)
                    elif i:
                        pe.wait_ge(evac, 7 * i)
                    th, tl = (t1_hi, t1_lo) if c == 6 else (t0_hi, t0_lo)
                    product(MIX_STEP * i + c * CP, pair(c % 2), th, tl,
                            ready=0 if i == 0 and c == 0 else None,
                            hook=lambda j: mixer_hook(i, c * CP + j))

            def turn_x(t, c, first):
                pe.wait_ge(resid, first + c + 1)
                pe.wait_ge(t_out, t)
                turn(pair(2), x_tok[:, :, c * W_GROUP:(c + 1) * W_GROUP])

            def w_out_hook(c, j):
                if c == 0 and j in (0, 3):
                    g = 2 + j // 3
                    pe.wait_ge(t_out, T_O + g)
                    pe.wait_ge(pt_out, GROUPS * HEADS)
                    pe.wait_ge(o_out, g + 1)
                    turn(pair(2), o_tok[:, :, g * W_GROUP:(g + 1) * W_GROUP])
                if c == 0 and j == 6:
                    pe.wait_ge(evac, 7 * GROUPS)
                    pe.wait_ge(t_out, T_KX)
                    turn(pair(2), kvx_tok[:, 0])
                if c and j == 2:
                    turn_x(T_WOUT + c - 1, c - 1, 0)

            pe.wait_ge(t_out, T_O + 2)
            for c in range(TG):
                if c == 1:
                    pe.wait_ge(evac, 7 * GROUPS)
                if c >= 2:
                    pe.wait_ge(resid, c - 1)
                product(P_WOUT + c * CP, pair((c + 1) % 2), t0_hi, t0_lo,
                        ready=T_O if c == 0 else None, hook=lambda j: w_out_hook(c, j))

            cross = GROUPS * HEADS

            def cross_scores(h):
                pe.wait_ge(evac, 7 * GROUPS + h + 1)
                if h == 0:
                    pe.wait_ge(t_out, T_XO)
                else:
                    pe.wait_ge(s_out, cross + h)
                for hf in range(HALVES):
                    mm = pe.matmul(pair(2)[:, 0, hf * S:(hf + 1) * S],
                                   lhsT=qT[:, 0, h, hf * P:(hf + 1) * P], rhs=kT[:, 0, h, :],
                                   start=True, stop=True)
                mm.then_inc(s_done, 1)

            def cross_probs(h):
                pe.wait_ge(diag_ready, h + 1)
                if h:
                    pe.wait_ge(pt_out, cross + h)
                for kt in range(2):
                    for hf in range(HALVES):
                        at = kt * S + hf * P
                        mm = pe.matmul(pair(2)[:, 1, at:at + P],
                                       lhsT=s_b[:, h % 2, hf * S + kt * P:hf * S + (kt + 1) * P],
                                       rhs=qk_tok[:, 0, h % 2, hf * P:(hf + 1) * P],
                                       start=True, stop=True)
                mm.then_inc(pt_done, 1)

            def cross_output(h):
                pe.wait_ge(pt_out, cross + h + 1)
                if h >= 2:
                    pe.wait_ge(o_out, 2 * GROUPS + h - 1)
                for kt in range(2):
                    mm = pe.matmul(pair(3)[:, h % 2, 0:S],
                                   lhsT=kvx_tok[:, 1, kt, h * HD:(h + 1) * HD],
                                   rhs=s_c[:, h % 2, kt * S:(kt + 1) * S],
                                   start=kt == 0, stop=kt == 1)
                mm.then_inc(heads_done, 1)

            pe.wait_ge(resid, TG - 1)
            for e, (h, half) in enumerate(XQ_PIECES):
                s = e % SLOTS
                pe.wait_ge(lo_ready, P_XQ + e + 1 + SLOTS)
                if half == 0:
                    pe.wait_ge(t_out, T_WOUT + 2)
                    if h >= 2:
                        pe.wait_ge(evac, 7 * GROUPS + h - 1)
                else:
                    pe.wait_ge(t_out, T_XO)
                q_bank = pair(1)[:, h % 2, 0:S]
                for kk in range(CP):
                    k = half * CP + kk
                    wh = w_hi[:, s, kk * P:(kk + 1) * P]
                    wl = w_lo[:, s, kk * P:(kk + 1) * P]
                    pe.matmul(q_bank, lhsT=wh, rhs=t1_hi[:, k, :], start=k == 0, stop=False)
                    pe.matmul(q_bank, lhsT=wh, rhs=t1_lo[:, k, :], start=False, stop=False)
                    mm = pe.matmul(q_bank, lhsT=wl, rhs=t1_hi[:, k, :], start=False,
                                   stop=k == KT - 1)
                mm.then_inc(piece_used, 1)
                if e == 0:
                    turn_x(T_WOUT + TG - 1, TG - 1, 0)
                if e == 3:
                    cross_scores(0)
                if e == 4:
                    cross_scores(1)
                if e == 5:
                    cross_probs(0)
                if e == 6:
                    cross_output(0)
                    cross_probs(1)
                    cross_scores(2)
                if e == 7:
                    cross_output(1)
                    cross_probs(2)
                    cross_scores(3)
                    cross_output(2)

            for e, (c, half) in enumerate(XO_PIECES):
                s = e % SLOTS
                if half == 0 and c >= 2:
                    pe.wait_ge(resid, TG + c - 1)
                if e in (0, 2):
                    pe.wait_ge(o_out, 2 * GROUPS + 2 * half + 2)
                pe.wait_ge(lo_ready, P_XO + e + 1 + SLOTS)
                for kk in range(2):
                    k = 2 * half + kk
                    wh = w_hi[:, s, kk * W_GROUP:(kk + 1) * W_GROUP]
                    wl = w_lo[:, s, kk * W_GROUP:(kk + 1) * W_GROUP]
                    for hf in range(HALVES):
                        th = t0_hi[:, k, hf * P:(hf + 1) * P]
                        tl = t0_lo[:, k, hf * P:(hf + 1) * P]
                        o = pair(c % 2)[:, hf, :]
                        pe.matmul(o, lhsT=th, rhs=wh, start=k == 0, stop=False)
                        pe.matmul(o, lhsT=th, rhs=wl, start=False, stop=False)
                        mm = pe.matmul(o, lhsT=tl, rhs=wh, start=False, stop=k == 3)
                mm.then_inc(piece_used, 1)
                if e == 0:
                    cross_probs(3)
                if e == 1:
                    cross_output(3)
                if e == 4:
                    pe.wait_ge(pt_out, cross + HEADS)
                if e in (4, 5, 7):
                    t = (4, 5, 7).index(e)
                    turn_x(T_XO + t, t, TG)
            product(P_GATE0, pair(0), t1_hi, t1_lo, ready=T_XO,
                    hook=lambda j: turn_x(T_XO + TG - 1, TG - 1, TG) if j == 1 else None)

            def turn_h(i):
                pe.wait_ge(h_ready, i + 2)
                pe.wait_ge(t_out, i + T_H)
                turn(pair(2), qk_tok[:, 1])

            pe.wait_ge(resid, 2 * TG)
            with pe.Fori(0, FC - 1) as i:
                pe.wait_ge(h_ready, i + 1)
                product(P_FFN + 2 * CP * i, pair(1), t1_hi, t1_lo)
                pe.wait_ge(silu_out, i + 1)
                product(P_FFN + 2 * CP * i + CP, pair(0), t1_hi, t1_lo,
                        hook=lambda j: turn_h(i) if j == 2 else None)
            pe.wait_ge(h_ready, FC)
            product(P_FFN + 2 * CP * (FC - 1), pair(1), t1_hi, t1_lo)

            def down_part(kk, j, q, hf, first=False, last=False):
                s = (2 * kk + j) % SLOTS
                wh = w_hi[:, s, q * W_GROUP:(q + 1) * W_GROUP]
                wl = w_lo[:, s, q * W_GROUP:(q + 1) * W_GROUP]
                o = down_bank(hf, 2 * j + q)
                th, tl = (h[:, kk, hf * P:(hf + 1) * P] for h in (h_hi, h_lo))
                pe.matmul(o, lhsT=th, rhs=wh, start=first, stop=False, skip_group_check=True)
                pe.matmul(o, lhsT=th, rhs=wl, start=False, stop=False, skip_group_check=True)
                return pe.matmul(o, lhsT=tl, rhs=wh, start=False, stop=last, skip_group_check=True)

            def down(i, tiles=SLOTS, first=False):
                for kk in range(tiles):
                    pe.wait_ge(h_split, SLOTS * i + kk + 1)
                    for j in range(2):
                        if first and kk == 0:
                            if j == 0:
                                pe.wait_ge(silu_out, FC)
                            else:
                                turn_h(FC - 1)
                                pe.wait_ge(t_out, T_END)
                        pe.wait_ge(lo_ready, DOWN_STEP * i + (P_DOWN + 2 * kk + j + 1 + SLOTS))
                        for q in range(2):
                            for hf in range(HALVES):
                                mm = down_part(kk, j, q, hf, first=first and kk == 0)
                        mm.then_inc(piece_used, 1)

            down(0, first=True)
            with pe.Fori(1, FK // SLOTS - 1) as i:
                down(i)
            down(FK // SLOTS - 1, tiles=SLOTS - 2)
            pe.wait_ge(h_split, FK)
            pe.wait_ge(lo_ready, P_END + SLOTS)
            for hf in range(HALVES):
                for c in range(TG):
                    for kk in (SLOTS - 2, SLOTS - 1):
                        mm = down_part(kk, c // 2, c % 2, hf, last=kk == SLOTS - 1)
                    mm.then_inc(bank_done, 1)


INPUTS = ["x", "mem", "positions", "g_mix", "w_in", "g_out_sb", "g_out_moba", "w_out", "g_xattn",
          "g_mem", "w_xq", "w_xkv", "w_xo", "g_ffn", "w_gate_up", "w_down", "g_final"]


def kernel(**inputs):
    import concourse.bacc as bacc
    from concourse.bass_utils import run_bass_kernel_spmd

    nc = bacc.Bacc("TRN2", target_bir_lowering=False, num_devices=1)
    arrays, args = {}, []
    for name in INPUTS:
        a = np.ascontiguousarray(inputs[name])
        arrays[f"in_{name}"] = a
        args.append(nc.dram_tensor(f"in_{name}", a.shape, mybir.dt.from_np(a.dtype),
                                   kind="ExternalInput").ap())
    out = nc.dram_tensor("out", (1, S, D), F32, kind="ExternalOutput").ap()
    build(nc, *args, out)
    return run_bass_kernel_spmd(nc, [arrays], core_ids=[0]).results[0]["out"]
```

```python
from contextlib import ExitStack

import numpy as np

import concourse.bass as bass
from concourse import mybir
from concourse.alu_op_type import AluOpType as ALU

F32 = mybir.dt.float32
F32R = mybir.dt.float32r
I32 = mybir.dt.int32
ACT = mybir.ActivationFunctionType
AX = mybir.AxisListType

P = 128
D = 2048
S = 256
HALVES = S // P
N_MEM = 256
HD = 128
W_GROUP = 512
HEADS = W_GROUP // HD
N_SB, N_MB = 8, 8
W_SB, W_MB = N_SB * HD, N_MB * HD
ROPE = HD // 4
RHALF = ROPE // 2
THETA = 500000.0
D_FF = ((8 * D + 3 * 256 - 1) // (3 * 256)) * 256
EPS = 1e-6
SCALE = HD ** -0.5
MASKED = -1e30

KT = D // P
PIECE = 1024
SLOTS = 4
CP = KT * W_GROUP // PIECE
TG = D // W_GROUP
LEAD = 3
GROUPS = W_SB // W_GROUP
FC = D_FF // W_GROUP
FK = D_FF // P
XP = W_GROUP * W_GROUP // P // PIECE

MIX_STEP = 7 * CP
P_WOUT = GROUPS * MIX_STEP
P_XQ = P_WOUT + TG * CP
P_XO = P_XQ + CP
P_GATE0 = P_XO + TG * XP
P_FFN = P_GATE0 + CP
P_DOWN = P_FFN + (2 * FC - 1) * CP
P_END = P_DOWN + 2 * FK
DOWN_STEP = 2 * SLOTS
DOWN_ORDER = [(kk, j) for kk in range(SLOTS) for j in range(2)]
DOWN_FIRST = [(0, 0), (1, 0), (0, 1), (1, 1)] + DOWN_ORDER[4:]

GAINED = [(hf, c) for hf in range(HALVES) for c in range(2)]

T_MEM = TG + 2
T_SB = [TG, T_MEM + TG + 2]
T_MB = [T_MEM + TG, T_MEM + TG + 4]
T_O = T_MB[1] + 2
T_KX = T_O + TG
T_WOUT = T_KX + 1
T_XO = T_WOUT + TG
T_H = T_XO + TG
T_END = T_H + FC

SPLIT_X, SPLIT_MEM, SPLIT_O, SPLIT_WOUT, SPLIT_XO = (TG * n for n in range(5))

NORM_X, NORM_MEM, NORM_HEADS = 0, 1, 2
NORM_Q = NORM_HEADS + 2 * GROUPS
NORM_F = NORM_Q + 1
NORM_OUT = NORM_F + 1

XQ_PIECES = [(0, 0), (1, 0), (0, 1), (1, 1), (2, 0), (2, 1), (3, 0), (3, 1)]
XO_PIECES = [(0, 0), (1, 0), (0, 1), (1, 1), (2, 0), (2, 1), (3, 0), (3, 1)]

G_MIX, G_MEM, G_X, G_FFN = 0, KT, 2 * KT, 3 * KT
G_O = 4 * KT
G_ROWS = G_O + KT

TRIG_STEPS = (2.0 ** 20, 2.0 ** 10, 1.0)


def split_two_pi():
    hi, lo = 6.283185307179586, 2.4492935982947064e-16
    parts, rest = [], hi
    for n in range(4):
        unit = 2.0 ** (2 - 11 * (n + 1))
        part = float(np.floor(rest / unit) * unit)
        parts.append(part)
        rest -= part
    return parts + [rest + lo]


class Chain:

    def __init__(self, engine, done, base=0):
        self.engine, self.done, self.base, self.n = engine, done, base, 0

    def __call__(self, instruction):
        self.n += 1
        instruction.then_inc(self.done, 1)
        self.engine.wait_ge(self.done, self.base + self.n)

    def at(self, base):
        self.base, self.n = base, 0


def build(nc, x, mem, positions, g_mix, w_in, g_out_sb, g_out_moba, w_out, g_xattn, g_mem,
          w_xq, w_xkv, w_xo, g_ffn, w_gate_up, w_down, g_final, out):
    place = [(nc.sbuf_base + 31) // 32 * 32]

    def sb(name, shape, dtype=F32, at=None):
        size = 4 * int(np.prod(shape[1:]))
        size = (size + 31) // 32 * 32
        if at is None:
            at = place[0]
            place[0] += size
            assert place[0] <= nc.sbuf_usable_end, (name, place[0])
        return nc.alloc_sbuf_tensor_at(name, shape, dtype, offset=at)

    x_tok = sb("x_tok", [P, HALVES, D])
    w_raw = sb("w_raw", [P, SLOTS, PIECE])
    w_hi = sb("w_hi", [P, SLOTS, PIECE], F32R)
    w_lo = sb("w_lo", [P, SLOTS, PIECE], F32R)
    t1_hi = sb("t1_hi", [P, KT, S], F32R)
    t1_lo = sb("t1_lo", [P, KT, S], F32R)
    t0_at = place[0]
    t0_hi = sb("t0_hi", [P, KT, S], F32R)
    t0_lo = sb("t0_lo", [P, KT, S], F32R)
    o_tok = sb("o_tok", [P, HALVES, D])
    hT = sb("hT", [P, FK, S], at=t0_at)
    assert t0_at + FK * S * 4 <= place[0]
    qkv_at = place[0]
    qT = sb("qT", [P, 2, HEADS, S])
    kT = sb("kT", [P, 2, HEADS, S])
    v_tok = sb("v_tok", [P, 2, HALVES, W_GROUP])
    h_hi = sb("h_hi", [P, SLOTS, S], F32R, at=qkv_at)
    h_lo = sb("h_lo", [P, SLOTS, S], F32R, at=qkv_at + SLOTS * S * 4)
    gfin = sb("gfin", [P, D], at=qkv_at + 2 * SLOTS * S * 4)
    qk_tok = sb("qk_tok", [P, 2, HALVES, W_GROUP])
    kvx_tok = sb("kvx_tok", [P, 2, HALVES, W_GROUP])
    s_a = sb("s_a", [P, 2, W_GROUP])
    s_b = sb("s_b", [P, 2, W_GROUP])
    s_c = sb("s_c", [P, 2, W_GROUP])
    ident = sb("ident", [P, P])
    neg_tri = sb("neg_tri", [P, P])
    neg_one = sb("neg_one", [P, P])
    causal = sb("causal", [P, 3 * P])
    past_one = sb("past_one", [P, 2 * P])
    ident_r = sb("ident_r", [P, P], F32R)
    not_past = sb("not_past", [P, 2 * P], F32R)
    g_rows = sb("g_rows", [G_ROWS, P])
    g_col = sb("g_col", [P, G_ROWS])
    pos_i = sb("pos_i", [P, HALVES], I32)
    pos_f = sb("pos_f", [P, HALVES])
    inv_freq = sb("inv_freq", [P, RHALF])
    ang = sb("ang", [P, HALVES * RHALF])
    turns = sb("turns", [P, HALVES * RHALF])
    cos_arg = sb("cos_arg", [P, HALVES * RHALF])
    sin_t = sb("sin_t", [P, HALVES, RHALF])
    cos_t = sb("cos_t", [P, HALVES, RHALF])
    rot = sb("rot", [P, 4, HALVES, HEADS * RHALF])
    ssq = sb("ssq", [P, 16])
    ms = sb("ms", [P, 8])
    ln_ms = sb("ln_ms", [P, 8])
    rs = sb("rs", [P, 8])
    nt = sb("nt", [P, 8])
    fac = sb("fac", [P, 8])
    rden = sb("rden", [P, 8])
    rowsum = sb("rowsum", [P, HALVES * HEADS])
    negmax = sb("negmax", [P, 2, HALVES])
    rstd_x = sb("rstd_x", [P, HALVES])
    rstd_m = sb("rstd_m", [P, HALVES])
    scale_q = sb("scale_q", [P, HALVES])
    rstd_f = sb("rstd_f", [P, HALVES])
    rstd_o = sb("rstd_o", [P, HALVES])
    wide = s_a[:, :, :].rearrange("p a b -> p (a b)")

    with ExitStack() as ctx:
        psum = ctx.enter_context(nc.psum_tensor("psum", [P, 8, 512], F32))

        def pair(n):
            return psum[:, 2 * n:2 * n + 2, :]

        def down_bank(hf, c):
            return psum[:, (2 * (c // 2) if hf == 0 else 6 - 2 * (c // 2)) + c % 2, :]

        def out_chunk(hf, c):
            return w_raw[:, 2 * hf + c // 2, (c % 2) * W_GROUP:(c % 2 + 1) * W_GROUP]

        def sem(name):
            return ctx.enter_context(nc.semaphore(name))

        x_landed = [sem(f"x_landed{c}") for c in range(TG)]
        mem_landed = [sem(f"mem_landed{c}") for c in range(TG)]
        g_mix_landed = sem("g_mix_landed")
        gains_landed = sem("gains_landed")
        pos_landed = sem("pos_landed")
        gfin_landed = sem("gfin_landed")
        raw_landed = [sem(f"raw_landed{s}") for s in range(SLOTS)]
        hi_ready = sem("hi_ready")
        lo_ready = sem("lo_ready")
        piece_used = sem("piece_used")
        ident_ready = sem("ident_ready")
        consts_ready = sem("consts_ready")
        gains_turned = sem("gains_turned")
        gains_ready = sem("gains_ready")
        t_done = sem("t_done")
        t_hi_ready = sem("t_hi_ready")
        t_out = sem("t_out")
        trig_args = sem("trig_args")
        trig_ready = sem("trig_ready")
        evac = sem("evac")
        ssq_ready = sem("ssq_ready")
        ms_ready = sem("ms_ready")
        root_ready = sem("root_ready")
        rstd_ready = sem("rstd_ready")
        rotated = sem("rotated")
        z_done = sem("z_done")
        log_ready = sem("log_ready")
        sp_ready = sem("sp_ready")
        sp_masked = sem("sp_masked")
        cum_done = sem("cum_done")
        w_exp = sem("w_exp")
        s_done = sem("s_done")
        s_out = sem("s_out")
        max_ready = sem("max_ready")
        p_ready = sem("p_ready")
        pt_done = sem("pt_done")
        pt_out = sem("pt_out")
        heads_done = sem("heads_done")
        o_out = sem("o_out")
        resid = sem("resid")
        silu_out = sem("silu_out")
        o_hi_ready = sem("o_hi_ready")
        diag_ready = sem("diag_ready")
        h_ready = sem("h_ready")
        h_hi_ready = sem("h_hi_ready")
        h_split = sem("h_split")
        bank_done = sem("bank_done")
        act_final = sem("act_final")
        dve_final = sem("dve_final")
        gained = sem("gained")
        rstd_o_ready = sem("rstd_o_ready")
        out_written = sem("out_written")
        act_step = sem("act_step")
        dve_step = sem("dve_step")
        pool_step = sem("pool_step")

        block = ctx.enter_context(nc.Block())

        gain_rows = [(g_mix, G_MIX), (g_mem, G_MEM), (g_xattn, G_X), (g_ffn, G_FFN),
                     (g_out_sb, G_O), (g_out_moba, G_O + W_SB // P)]

        @block.sync
        def _(sp):
            def load(n, s, src):
                sp.wait_ge(lo_ready, n + 1)
                dst = w_raw[:, s, :]
                if len(src.shape) == 3:
                    dst = dst.rearrange("p (t c) -> p t c", t=src.shape[1])
                sp.dma_start(dst, src).then_inc(raw_landed[s], 16)

            def load_chunk(n, w, col, hook=None):
                for j in range(CP):
                    rows = w[2 * j * P:(2 * j + 2) * P, bass.ds(col, W_GROUP)]
                    load(n + j, j % SLOTS, rows.rearrange("(t p) c -> p t c", p=P))
                    if hook and j < TG - 1:
                        hook(j + 1)

            def load_x(c):
                cols = slice(c * W_GROUP, (c + 1) * W_GROUP)
                sp.dma_start(x_tok[:, :, cols], x[0, :, cols].rearrange("(h p) c -> p h c", p=P)) \
                    .then_inc(x_landed[c], 16)

            load_x(0)
            for i in range(GROUPS):
                for c in range(6):
                    load_chunk(MIX_STEP * i + c * CP, w_in, W_GROUP * i + c * W_SB,
                               hook=load_x if i == 0 and c == 0 else None)
                load_chunk(MIX_STEP * i + 6 * CP, w_xkv, W_GROUP * i)
            with sp.Fori(0, TG) as i:
                load_chunk(P_WOUT + CP * i, w_out, W_GROUP * i)
            for e, (h, half) in enumerate(XQ_PIECES):
                rows = w_xq[half * D // 2:(half + 1) * D // 2, h * HD:(h + 1) * HD]
                load(P_XQ + e, e % SLOTS, rows.rearrange("(t p) c -> p t c", p=P))
            for e, (c, half) in enumerate(XO_PIECES):
                rows = w_xo[2 * half * P:(2 * half + 2) * P, c * W_GROUP:(c + 1) * W_GROUP]
                load(P_XO + e, e % SLOTS, rows.rearrange("(t p) c -> p t c", p=P))
            load_chunk(P_GATE0, w_gate_up, 0)
            with sp.Fori(0, FC - 1) as i:
                load_chunk(P_FFN + 2 * CP * i, w_gate_up, D_FF + W_GROUP * i)
                load_chunk(P_FFN + 2 * CP * i + CP, w_gate_up, W_GROUP * i + W_GROUP)
            load_chunk(P_FFN + 2 * CP * (FC - 1), w_gate_up, 2 * D_FF - W_GROUP)

            def load_down(i, order):
                for e, (kk, j) in enumerate(order):
                    rows = w_down[bass.ds(SLOTS * P * i + kk * P, P), j * PIECE:(j + 1) * PIECE]
                    load(P_DOWN + DOWN_STEP * i + e, e % SLOTS, rows)

            load_down(0, DOWN_FIRST)
            with sp.Fori(1, FK // SLOTS) as i:
                load_down(i, DOWN_ORDER)
            for hf in range(HALVES):
                for c, done in ((0, act_final), (2, dve_final), (1, act_final), (3, dve_final)):
                    sp.wait_ge(done, 2 * hf + c % 2 + 1)
                    sp.dma_start(out[0, hf * P:(hf + 1) * P, c * W_GROUP:(c + 1) * W_GROUP],
                                 out_chunk(hf, c)).then_inc(out_written, 16)
            sp.wait_ge(out_written, 16 * HALVES * TG)

        @block.gpsimd
        def _(pool):
            chain = Chain(pool, pool_step)
            chain(pool.memset(ident[:, :], 0.0))
            pool.affine_select(out=ident[:, :], in_=ident[:, :], compare_op=ALU.not_equal, fill=1.0,
                               base=0, pattern=[[-1, P]], channel_multiplier=1) \
                .then_inc(ident_ready, 1)
            for g, at in gain_rows[1:]:
                n = g.shape[0] // P
                pool.dma_start(g_rows[at:at + n, :], g.rearrange("(t p) -> t p", p=P)) \
                    .then_inc(gains_landed, 16)
            pool.dma_start(pos_i[:, :], positions[0, :].rearrange("(h p) -> p h", p=P),
                           allow_slow_non_contiguous=True).then_inc(pos_landed, 16)
            for b in range(RHALF):
                pool.memset(inv_freq[:, b:b + 1], float(np.float32(THETA ** (-2.0 * b / ROPE))))
            pool.memset(neg_one[:, :], -1.0)
            pool.memset(neg_tri[:, :], -1.0)
            pool.memset(causal[:, :], 0.0)
            chain(pool.memset(past_one[:, :], 1.0))
            pool.wait_ge(ident_ready, 1)
            pool.affine_select(out=neg_tri[:, :], in_=neg_tri[:, :], compare_op=ALU.is_ge, fill=0.0,
                               base=0, pattern=[[-1, P]], channel_multiplier=1)
            diag = causal[:, 0:2 * P].rearrange("p (b t) -> p b t", b=2)
            pool.affine_select(out=diag, in_=diag, compare_op=ALU.is_ge, fill=MASKED,
                               base=0, pattern=[[0, 2], [-1, P]], channel_multiplier=1)
            past, not_yet = (t[:, :].rearrange("p (b t) -> p b t", b=2) for t in (past_one, not_past))
            zeros = causal[:, 2 * P:3 * P].unsqueeze(1).to_broadcast([P, 2, P])
            for src, dst, fill in ((past, past, 0.0), (zeros, not_yet, MASKED)):
                ins = pool.affine_select(out=dst, in_=src, compare_op=ALU.is_ge, fill=fill,
                                         base=-1, pattern=[[0, 2], [1, P]], channel_multiplier=-1)
            chain(ins)
            pool.tensor_copy(ident_r[:, :], ident[:, :]).then_inc(consts_ready, 1)

            pool.wait_ge(pos_landed, 16)
            chain(pool.tensor_copy(pos_f[:, :], pos_i[:, :]))
            for hf in range(HALVES):
                ins = pool.tensor_scalar(ang[:, hf * RHALF:(hf + 1) * RHALF], inv_freq[:, :],
                                         pos_f[:, hf:hf + 1], None, ALU.mult)
            chain(ins)
            magic = 1.5 * 2.0 ** 23
            for scale in TRIG_STEPS:
                chain(pool.tensor_scalar(turns[:, :], ang[:, :], 1.0 / (2 * np.pi * scale), None,
                                         ALU.mult))
                chain(pool.tensor_scalar(turns[:, :], turns[:, :], magic, None, ALU.add))
                chain(pool.tensor_scalar(turns[:, :], turns[:, :], -magic, None, ALU.add))
                for part in split_two_pi():
                    chain(pool.tensor_scalar(cos_arg[:, :], turns[:, :], part * scale, None,
                                             ALU.mult))
                    chain(pool.tensor_tensor(ang[:, :], ang[:, :], cos_arg[:, :], ALU.subtract))
            below_pi = 3.1415925
            chain(pool.tensor_scalar(ang[:, :], ang[:, :], below_pi, None, ALU.min))
            chain(pool.tensor_scalar(ang[:, :], ang[:, :], -below_pi, None, ALU.max))
            pool.tensor_scalar(cos_arg[:, :], ang[:, :], 0.0, None, ALU.max)
            chain(pool.tensor_scalar(turns[:, :], ang[:, :], 0.0, None, ALU.min))
            chain(pool.tensor_tensor(cos_arg[:, :], cos_arg[:, :], turns[:, :], ALU.subtract))
            pool.tensor_scalar(cos_arg[:, :], cos_arg[:, :], -1.0, np.pi / 2, ALU.mult, ALU.add) \
                .then_inc(trig_args, 1)
            pool.wait_ge(trig_ready, 1)

            def rotate(which):
                v = qk_tok[:, which, :, :].rearrange("p h (n d) -> p h n d", n=HEADS)
                x1, x2 = v[:, :, :, 0:RHALF], v[:, :, :, RHALF:ROPE]
                shape = [P, HALVES, HEADS, RHALF]
                cos, sin = (t[:, :, :].unsqueeze(2).to_broadcast(shape) for t in (cos_t, sin_t))
                r = [rot[:, n, :, :].rearrange("p h (n d) -> p h n d", n=HEADS) for n in range(4)]
                pool.tensor_tensor(r[0], x1, cos, ALU.mult)
                pool.tensor_tensor(r[1], x2, sin, ALU.mult)
                pool.tensor_tensor(r[2], x2, cos, ALU.mult)
                chain(pool.tensor_tensor(r[3], x1, sin, ALU.mult))
                pool.tensor_tensor(x1, r[0], r[1], ALU.subtract)
                pool.tensor_tensor(x2, r[2], r[3], ALU.add).then_inc(rotated, 1)

            steps = 2
            start = chain.n
            with pool.Fori(0, GROUPS) as i:
                chain.at(start + steps * i)
                for h in range(HEADS):
                    pool.wait_ge(sp_ready, HEADS * i + h + 1)
                    pool.tensor_tensor(s_a[:, h % 2, 0:2 * P], s_a[:, h % 2, 0:2 * P],
                                       past_one[:, :], ALU.mult).then_inc(sp_masked, 1)
                    if h in (1, 3):
                        pool.wait_ge(evac, 7 * i + 4 + h // 2)
                        rotate(h // 2)
                assert chain.n == steps

            pool.wait_ge(gfin_landed, 16)
            for hf, c in GAINED:
                cols = slice(c * W_GROUP, (c + 1) * W_GROUP)
                pool.wait_ge(resid, 2 * TG + hf * TG + c + 1)
                pool.tensor_tensor(out_chunk(hf, c), x_tok[:, hf, cols], gfin[:, cols], ALU.mult) \
                    .then_inc(gained, 1)

        @block.scalar
        def _(act):
            chain = Chain(act, act_step)

            def hi(n, s):
                act.wait_ge(raw_landed[s], 4 * n + (16 - 4 * s))
                act.wait_ge(piece_used, n + 1)
                act.copy(w_hi[:, s, :], w_raw[:, s, :]).then_inc(hi_ready, 1)

            def turned_hi(t, dst, tile0, gain0, banks):
                act.wait_ge(t_done, t + 1)
                for b in range(2):
                    for kk in (2 * b, 2 * b + 1):
                        ins = act.activation(dst[:, tile0 + kk, :],
                                             banks[:, b, (kk % 2) * S:(kk % 2 + 1) * S], ACT.Copy,
                                             scale=g_col[:, gain0 + kk:gain0 + kk + 1])
                    ins.then_inc(t_hi_ready, 1)

            def evacuate(n_end, banks, dst, rstd):
                act.wait_ge(piece_used, n_end + SLOTS)
                for hf in range(HALVES):
                    ins = act.activation(dst[:, hf, :], banks[:, hf, :], ACT.Copy,
                                         scale=rstd[:, hf:hf + 1])
                ins.then_inc(evac, 1)

            def inverse_root(norm, cols):
                act.wait_ge(ms_ready, norm + 1)
                chain(act.activation(ln_ms[:, 0:cols], ms[:, 0:cols], ACT.Ln))
                act.activation(rs[:, 0:cols], ln_ms[:, 0:cols], ACT.Exp, scale=-0.5) \
                    .then_inc(root_ready, 1)

            def square_heads(group):
                act.wait_ge(heads_done, group + 1)
                for hf in range(HALVES):
                    ins = act.activation(s_a[:, hf, :], pair(3)[:, hf, :], ACT.Square)
                ins.then_inc(ssq_ready, 1)

            def exponentials(n, h, src, half_cols, scales):
                act.wait_ge(max_ready, n + 1)
                b = h % 2
                for hf, cols in enumerate(half_cols):
                    ins = act.activation(s_b[:, b, cols], src[:, cols], ACT.Exp,
                                         bias=negmax[:, b, hf:hf + 1], scale=scales[hf],
                                         accum_out=rowsum[:, hf * HEADS + h:hf * HEADS + h + 1])
                ins.then_inc(p_ready, 1)

            def square_input(norm, src, part):
                hf, q = part // 2, part % 2
                at = 4 * norm + part
                chain(act.activation(wide, src[:, hf, q * PIECE:(q + 1) * PIECE], ACT.Square,
                                     accum_out=ssq[:, at:at + 1]))
                if part == 3:
                    act.sem_inc(ssq_ready, 1)

            act.dma_start(g_rows[0:KT, :], g_mix.rearrange("(t p) -> t p", p=P)) \
                .then_inc(g_mix_landed, 16)
            act.preload_act_table_set("natural_log_exp_and_others")
            act.wait_ge(gains_ready, 1)
            turned_hi(0, t0_hi, 0, G_MIX, pair(2))
            for c in range(TG):
                cols = slice(c * W_GROUP, (c + 1) * W_GROUP)
                act.dma_start(o_tok[:, :, cols], mem[0, :, cols].rearrange("(h p) c -> p h c", p=P)) \
                    .then_inc(mem_landed[c], 16)
            hi(0, 0)
            hi(1, 1)
            turned_hi(1, t0_hi, 4, G_MIX + 4, pair(3))
            hi(2, 2)

            for i in range(GROUPS):
                n0 = MIX_STEP * i
                for s in range(MIX_STEP):
                    hi(n0 + s + LEAD, (s + LEAD) % SLOTS)
                    if i == 0:
                        if s in (0, 2):
                            c = 2 + s // 2
                            turned_hi(c, t0_hi, 4 * c, G_MIX + 4 * c, pair(c))
                        if s in (1, 3, 4, 5):
                            square_input(NORM_X, x_tok, (1, 3, 4, 5).index(s))
                        if 19 <= s < 23:
                            c = s - 19
                            if c == 0:
                                act.wait_ge(gains_ready, 2)
                            turned_hi(T_MEM + c, t1_hi, 4 * c, G_MEM + 4 * c, pair(2 + c % 2))
                        if s == 6:
                            inverse_root(NORM_X, HALVES)
                            act.wait_ge(rstd_ready, 1)
                        if 9 <= s < 13:
                            if s < 11:
                                act.wait_ge(mem_landed[2 * (s - 9)], 16)
                                act.wait_ge(mem_landed[2 * (s - 9) + 1], 16)
                            square_input(NORM_MEM, o_tok, s - 9)
                        if s == 14:
                            inverse_root(NORM_MEM, HALVES)
                            act.wait_ge(rstd_ready, 2)
                        if s == 16:
                            act.wait_ge(trig_args, 1)
                            act.activation(sin_t[:, :, :].rearrange("p h f -> p (h f)"), ang[:, :],
                                           ACT.Sin)
                            act.activation(cos_t[:, :, :].rearrange("p h f -> p (h f)"),
                                           cos_arg[:, :], ACT.Sin).then_inc(trig_ready, 1)
                            act.preload_act_table_set("natural_log_exp_and_others")
                    if s % CP == CP - 1:
                        c = s // CP
                        dst = [qk_tok[:, 0], qk_tok[:, 1], v_tok[:, 0], qk_tok[:, 0],
                               qk_tok[:, 1], v_tok[:, 1], kvx_tok[:, i]][c]
                        evacuate(n0 + s + 1, pair(c % 2), dst, rstd_m if c == 6 else rstd_x)
                    for h in range(HEADS):
                        if s == 3 * CP + 4 * h:
                            b = h % 2
                            act.wait_ge(z_done, HEADS * i + h + 1)
                            chain(act.activation(s_b[:, b, 0:384], pair(2)[:, b, 0:384], ACT.Abs))
                            chain(act.activation(s_b[:, b, 0:384], s_b[:, b, 0:384], ACT.Exp,
                                                 scale=-1.0))
                            act.activation(s_b[:, b, 0:384], s_b[:, b, 0:384], ACT.Ln, bias=1.0) \
                                .then_inc(log_ready, 1)
                        if s == 3 * CP + 4 * h + 3:
                            act.wait_ge(cum_done, HEADS * i + h + 1)
                            act.activation(s_c[:, h % 2, 0:384], pair(2)[:, h % 2, 0:384], ACT.Exp) \
                                .then_inc(w_exp, 1)
                        if s == 46 + 2 * h:
                            exponentials(HEADS * i + h, h, s_a[:, h % 2, :],
                                         (slice(0, P), slice(P, 3 * P)), (SCALE, SCALE))
                    if s == 42:
                        square_heads(2 * i)
                    if s == 43:
                        inverse_root(NORM_HEADS + 2 * i, 8)
                    if i == GROUPS - 1 and s in (50, 53):
                        c = (s - 50) // 3
                        turned_hi(T_O + c, t0_hi, 4 * c, G_O + 4 * c, pair(1))
                    if s == 55:
                        square_heads(2 * i + 1)
                        inverse_root(NORM_HEADS + 2 * i + 1, 8)

            def square_chunk(first, c):
                act.wait_ge(resid, first + c + 1)
                for hf in range(HALVES):
                    at = hf * TG + c
                    chain(act.activation(wide[:, 0:W_GROUP],
                                         x_tok[:, hf, c * W_GROUP:(c + 1) * W_GROUP],
                                         ACT.Square, accum_out=ssq[:, at:at + 1]))
                if c == TG - 1:
                    act.sem_inc(ssq_ready, 1)

            for s in range(TG * CP):
                n = P_WOUT + s + LEAD
                hi(n, n % SLOTS)
                if s in (0, 3):
                    c = 2 + s // 3
                    turned_hi(T_O + c, t0_hi, 4 * c, G_O + 4 * c, pair(2))
                if s % CP == CP - 1:
                    square_chunk(0, s // CP)
                if s >= CP and s % CP == 2:
                    c = s // CP - 1
                    turned_hi(T_WOUT + c, t1_hi, 4 * c, G_X + 4 * c, pair(2))

            def q_copy(h, e):
                act.wait_ge(piece_used, P_XQ + e + 1 + SLOTS)
                act.copy(qT[:, 0, h, :], pair(1)[:, h % 2, 0:S]).then_inc(evac, 1)

            def head_hi(h):
                act.wait_ge(heads_done, 2 * GROUPS + h + 1)
                act.copy(t0_hi[:, h, :], pair(3)[:, h % 2, 0:S]).then_inc(o_hi_ready, 1)

            def cross_exps(h):
                exponentials(GROUPS * HEADS + h, h, pair(2)[:, 0, :],
                             (slice(0, S), slice(S, 2 * S)),
                             [scale_q[:, hf:hf + 1] for hf in range(HALVES)])

            for s in range(CP):
                n = P_XQ + s + LEAD
                hi(n, n % SLOTS)
                if s == 0:
                    turned_hi(T_WOUT + TG - 1, t1_hi, KT - 4, G_X + KT - 4, pair(2))
                if s == 1:
                    inverse_root(NORM_Q, HALVES)
                    act.wait_ge(rstd_ready, 3)
                if s == 3:
                    q_copy(0, 2)
                if s == 4:
                    q_copy(1, 3)
                    cross_exps(0)
                if s == 5:
                    cross_exps(1)
                if s == 6:
                    q_copy(2, 5)
                    head_hi(0)
                if s == 7:
                    cross_exps(2)
                    head_hi(1)
            for s in range(TG * XP):
                n = P_XO + s + LEAD
                if s == 0:
                    q_copy(3, 7)
                if s == 2:
                    head_hi(3)
                hi(n, n % SLOTS)
                if s == 0:
                    cross_exps(3)
                if s == 1:
                    head_hi(2)
                if XO_PIECES[s][1] == 1:
                    square_chunk(TG, XO_PIECES[s][0])
                if s in (4, 5, 7):
                    c = (4, 5, 7).index(s)
                    turned_hi(T_XO + c, t1_hi, 4 * c, G_FFN + 4 * c, pair(2 + c % 2))
            for s in range(CP):
                n = P_GATE0 + s + LEAD
                hi(n, n % SLOTS)
                if s == 1:
                    turned_hi(T_XO + TG - 1, t1_hi, KT - 4, G_FFN + KT - 4, pair(3))
                    inverse_root(NORM_F, HALVES)
            act.wait_ge(rstd_ready, 4)
            act.preload_act_table_set("silu_and_others")

            def silu(i, n_end):
                act.wait_ge(piece_used, n_end + SLOTS)
                act.wait_ge(h_ready, i + 1)
                for hf in range(HALVES):
                    ins = act.activation(qk_tok[:, 0, hf, :], pair(0)[:, hf, :], ACT.Silu,
                                         scale=rstd_f[:, hf:hf + 1])
                ins.then_inc(silu_out, 1)

            with act.Fori(0, FC - 1) as i:
                for s in range(2 * CP):
                    n = P_FFN + 2 * CP * i + s
                    hi(n + LEAD, (s + LEAD) % SLOTS)
                    if s == 0:
                        silu(i, n)
            for s in range(CP):
                n = P_FFN + 2 * CP * (FC - 1) + s
                hi(n + LEAD, (s + LEAD) % SLOTS)
                if s == 0:
                    silu(FC - 1, n)

            def h_upper(k, s):
                act.wait_ge(piece_used, 2 * k + (P_DOWN + SLOTS - 2 * SLOTS + 3))
                act.copy(h_hi[:, s, :], hT[:, bass.ds(k, 1), :].rearrange("p k t -> p (k t)")) \
                    .then_inc(h_hi_ready, 1)

            def down(i, first=False, last=False):
                for j in range(DOWN_STEP):
                    if j % 2 == 0 and not (first and j == 0) and not (last and j == DOWN_STEP - 2):
                        h_upper(SLOTS * i + j // 2 + 1, (j // 2 + 1) % SLOTS)
                    if not (last and j >= DOWN_STEP - LEAD):
                        hi(P_DOWN + LEAD + DOWN_STEP * i + j, (j + LEAD) % SLOTS)

            act.wait_ge(t_out, T_END - 1)
            act.dma_start(gfin[:, :], g_final.partition_broadcast(P)).then_inc(gfin_landed, 16)
            h_upper(0, 0)
            h_upper(1, 1)
            act.preload_act_table_set("natural_log_exp_and_others")
            down(0, first=True)
            with act.Fori(1, FK // SLOTS - 1) as i:
                down(i)
            down(FK // SLOTS - 1, last=True)

            def finish(hf, c):
                act.wait_ge(rstd_o_ready, hf + 1)
                act.wait_ge(gained, 2 * hf + c + 1)
                act.activation(out_chunk(hf, c), out_chunk(hf, c), ACT.Copy,
                               scale=rstd_o[:, hf:hf + 1]).then_inc(act_final, 1)

            for hf in range(HALVES):
                for c in range(TG):
                    if hf == 1 and c in (1, 2):
                        finish(0, c - 1)
                    act.wait_ge(resid, 2 * TG + hf * TG + c + 1)
                    ins = act.activation(wide[:, 0:W_GROUP],
                                         x_tok[:, hf, c * W_GROUP:(c + 1) * W_GROUP],
                                         ACT.Square, accum_out=ssq[:, hf * TG + c:hf * TG + c + 1])
                    chain(ins)
                act.sem_inc(ssq_ready, 1)
                inverse_root(NORM_OUT + hf, 1)
            finish(1, 0)
            finish(1, 1)

        @block.vector
        def _(dve):
            chain = Chain(dve, dve_step)

            def lo(n, s):
                dve.wait_ge(hi_ready, n + 1)
                dve.tensor_tensor(w_lo[:, s, :], w_raw[:, s, :], w_hi[:, s, :].bitcast(F32),
                                  ALU.subtract).then_inc(lo_ready, 1)

            def turned_lo(group, dst, dst_hi, tile0, gain0, banks):
                for b in range(2):
                    dve.wait_ge(t_hi_ready, 2 * group + b + 1)
                    for kk in (2 * b, 2 * b + 1):
                        ins = dve.scalar_tensor_tensor(
                            out=dst[:, tile0 + kk, :],
                            in0=banks[:, b, (kk % 2) * S:(kk % 2 + 1) * S],
                            scalar=g_col[:, gain0 + kk:gain0 + kk + 1],
                            in1=dst_hi[:, tile0 + kk, :].bitcast(F32),
                            op0=ALU.mult, op1=ALU.subtract)
                ins.then_inc(t_out, 1)

            def turned_out(t, dst, scale):
                dve.wait_ge(t_done, t + 1)
                for b in range(2):
                    ins = dve.tensor_scalar(
                        dst[:, 2 * b:2 * b + 2, :].rearrange("p n t -> p (n t)"),
                        pair(2)[:, b, :], scale, None, ALU.mult)
                ins.then_inc(t_out, 1)

            def refine(norm, cols, dst):
                dve.wait_ge(root_ready, norm + 1)
                y, m, t = rs[:, 0:cols], ms[:, 0:cols], nt[:, 0:cols]
                chain(dve.tensor_tensor(t, y, y, ALU.mult))
                chain(dve.tensor_tensor(t, t, m, ALU.mult))
                chain(dve.tensor_scalar(t, t, -0.5, 1.5, ALU.mult, ALU.add))
                return dve.tensor_tensor(dst, y, t, ALU.mult)

            def head_squares(norm, softmax):
                if softmax:
                    chain(dve.reciprocal(rden[:, 0:8], rowsum[:, :]))
                    dve.tensor_tensor(fac[:, 0:8], rden[:, 0:8], rden[:, 0:8], ALU.mult)
                dve.wait_ge(ssq_ready, norm + 1)
                for hf in range(HALVES):
                    ins = dve.tensor_reduce(ssq[:, hf * HEADS:(hf + 1) * HEADS],
                                            s_a[:, hf, :].rearrange("p (n d) -> p n d", n=HEADS),
                                            AX.X, ALU.add)
                chain(ins)
                if softmax:
                    chain(dve.tensor_tensor(ssq[:, 0:8], ssq[:, 0:8], fac[:, 0:8], ALU.mult))
                dve.tensor_scalar(ms[:, 0:8], ssq[:, 0:8], 1.0 / HD, EPS, ALU.mult, ALU.add) \
                    .then_inc(ms_ready, 1)

            def head_outputs(norm, softmax, col):
                chain(refine(norm, 8, fac[:, 0:8]))
                if softmax:
                    chain(dve.tensor_tensor(fac[:, 0:8], fac[:, 0:8], rden[:, 0:8], ALU.mult))
                scale_heads(o_tok, col)

            def scale_heads(dst, col):
                for hf in range(HALVES):
                    f = fac[:, hf * HEADS:(hf + 1) * HEADS].unsqueeze(2).to_broadcast([P, HEADS, HD])
                    ins = dve.tensor_tensor(
                        dst[:, hf, bass.ds(col, W_GROUP)].rearrange("p (n d) -> p n d", n=HEADS),
                        pair(3)[:, hf, :].rearrange("p (n d) -> p n d", n=HEADS), f, ALU.mult)
                ins.then_inc(o_out, 1)

            def masked_maxima(n, h):
                b = h % 2
                dve.wait_ge(s_done, n + 1)
                dve.tensor_tensor(s_a[:, b, 0:3 * P], pair(2)[:, 0, 0:3 * P], causal[:, :],
                                  ALU.add).then_inc(s_out, 1)
                dve.wait_ge(s_out, n + 1)
                dve.tensor_reduce(negmax[:, b, 0:1], s_a[:, b, 0:P], AX.X, ALU.max)
                chain(dve.tensor_reduce(negmax[:, b, 1:2], s_a[:, b, P:3 * P], AX.X, ALU.max))
                dve.tensor_scalar(negmax[:, b, :], negmax[:, b, :], -SCALE, None, ALU.mult) \
                    .then_inc(max_ready, 1)

            def cross_maxima(h):
                b = h % 2
                dve.wait_ge(s_done, GROUPS * HEADS + h + 1)
                chain(dve.tensor_reduce(negmax[:, b, :],
                                        pair(2)[:, 0, :].rearrange("p (n k) -> p n k", n=HALVES),
                                        AX.X, ALU.max))
                dve.scalar_tensor_tensor(out=negmax[:, b, :], in0=negmax[:, b, :], scalar=-1.0,
                                         in1=scale_q[:, :], op0=ALU.mult, op1=ALU.mult) \
                    .then_inc(max_ready, 1)

            def probs_out(n, h, width):
                dve.wait_ge(pt_done, n + 1)
                dve.tensor_copy(s_c[:, h % 2, 0:width], pair(2)[:, 1, 0:width]).then_inc(pt_out, 1)

            def row_ms(norm, cols, cuts, first=0):
                dve.wait_ge(ssq_ready, norm + 1)
                part = ssq[:, first:first + cols * cuts]
                chain(dve.tensor_reduce(nt[:, 0:cols], part.rearrange("p (n c) -> p n c", c=cuts),
                                        AX.X, ALU.add))
                dve.tensor_scalar(ms[:, 0:cols], nt[:, 0:cols], 1.0 / D, EPS, ALU.mult, ALU.add) \
                    .then_inc(ms_ready, 1)

            dve.sem_inc(lo_ready, SLOTS)
            dve.sem_inc(h_ready, 1)

            dve.wait_ge(gains_turned, 1)
            dve.tensor_copy(g_col[:, 0:KT], psum[:, 0, 0:KT]).then_inc(gains_ready, 1)
            dve.wait_ge(gains_ready, 1)
            turned_lo(0, t0_lo, t0_hi, 0, G_MIX, pair(2))
            lo(0, 0)
            lo(1, 1)
            turned_lo(1, t0_lo, t0_hi, 4, G_MIX + 4, pair(3))
            lo(2, 2)

            for i in range(GROUPS):
                n0 = MIX_STEP * i
                for s in range(MIX_STEP):
                    lo(n0 + s + LEAD, (s + LEAD) % SLOTS)
                    if i == 0:
                        if s in (0, 2):
                            c = 2 + s // 2
                            turned_lo(c, t0_lo, t0_hi, 4 * c, G_MIX + 4 * c, pair(c))
                        if s == 11:
                            dve.wait_ge(gains_turned, 2)
                            dve.tensor_copy(g_col[:, KT:G_ROWS], pair(3)[:, 0, KT:G_ROWS]) \
                                .then_inc(gains_ready, 1)
                            dve.wait_ge(gains_ready, 2)
                        if 19 <= s < 23:
                            c = s - 19
                            turned_lo(SPLIT_MEM + c, t1_lo, t1_hi, 4 * c, G_MEM + 4 * c,
                                      pair(2 + c % 2))
                        if s == 6:
                            row_ms(NORM_X, HALVES, 2)
                            refine(NORM_X, HALVES, rstd_x[:, :]).then_inc(rstd_ready, 1)
                        if s == 14:
                            row_ms(NORM_MEM, HALVES, 2, first=4)
                            refine(NORM_MEM, HALVES, rstd_m[:, :]).then_inc(rstd_ready, 1)
                    if s == CP + 2:
                        turned_out(T_SB[i], qT[:, 0], SCALE)
                    if s == 2 * CP + 2:
                        turned_out(T_SB[i] + 1, kT[:, 0], 1.0)
                    for h in range(HEADS):
                        if s == 3 * CP + 4 * h + 1:
                            b = h % 2
                            dve.wait_ge(log_ready, HEADS * i + h + 1)
                            dve.scalar_tensor_tensor(out=s_a[:, b, 0:384],
                                                     in0=pair(2)[:, b, 0:384], scalar=0.0,
                                                     in1=s_b[:, b, 0:384], op0=ALU.max,
                                                     op1=ALU.add).then_inc(sp_ready, 1)
                        if s == 46 + 2 * h:
                            masked_maxima(HEADS * i + h, h)
                        if s == 48 + 2 * h:
                            probs_out(HEADS * i + h, h, 3 * P)
                    if s == 42:
                        turned_out(T_MB[i], qT[:, 1], 1.0)
                    if s == 43:
                        head_squares(NORM_HEADS + 2 * i, False)
                    if s == 44:
                        head_outputs(NORM_HEADS + 2 * i, False, W_GROUP * i)
                        turned_out(T_MB[i] + 1, kT[:, 1], 1.0)
                    if i == GROUPS - 1 and s in (50, 53):
                        c = (s - 50) // 3
                        turned_lo(SPLIT_O + c, t0_lo, t0_hi, 4 * c, G_O + 4 * c, pair(1))
                    if s == 55:
                        head_squares(NORM_HEADS + 2 * i + 1, True)
                        head_outputs(NORM_HEADS + 2 * i + 1, True, W_SB + W_GROUP * i)

            def add_residual(n_end, banks, c):
                dve.wait_ge(piece_used, n_end + SLOTS)
                for hf in range(HALVES):
                    x_part = x_tok[:, hf, c * W_GROUP:(c + 1) * W_GROUP]
                    ins = dve.tensor_tensor(x_part, banks[:, hf, :], x_part, ALU.add)
                ins.then_inc(resid, 1)

            for s in range(TG * CP):
                n = P_WOUT + s + LEAD
                lo(n, n % SLOTS)
                if s in (0, 3):
                    c = 2 + s // 3
                    turned_lo(SPLIT_O + c, t0_lo, t0_hi, 4 * c, G_O + 4 * c, pair(2))
                if s == 6:
                    turned_out(T_KX, kT[:, 0], 1.0)
                if s % CP == CP - 1:
                    add_residual(P_WOUT + s + 1, pair((s // CP + 1) % 2), s // CP)
                if s >= CP and s % CP == 2:
                    c = s // CP - 1
                    turned_lo(SPLIT_WOUT + c, t1_lo, t1_hi, 4 * c, G_X + 4 * c, pair(2))

            def diagonals(h):
                dve.wait_ge(p_ready, cross + h + 1)
                inv = rden[:, 2 * (h % 2):2 * (h % 2) + 2]
                sums = rowsum[:, :].rearrange("p (a b) -> p a b", b=HEADS)[:, :, h]
                chain(dve.reciprocal(inv, sums))
                for hf in range(HALVES):
                    ins = dve.tensor_scalar(qk_tok[:, 0, h % 2, hf * P:(hf + 1) * P], ident[:, :],
                                            inv[:, hf:hf + 1], None, ALU.mult)
                ins.then_inc(diag_ready, 1)

            def head_lo(h):
                dve.wait_ge(o_hi_ready, h + 1)
                dve.tensor_tensor(t0_lo[:, h, :], pair(3)[:, h % 2, 0:S],
                                  t0_hi[:, h, :].bitcast(F32), ALU.subtract).then_inc(o_out, 1)

            cross = GROUPS * HEADS
            for s in range(CP):
                n = P_XQ + s + LEAD
                if s == 4:
                    cross_maxima(0)
                if s == 5:
                    diagonals(0)
                    cross_maxima(1)
                lo(n, n % SLOTS)
                if s == 0:
                    turned_lo(SPLIT_WOUT + TG - 1, t1_lo, t1_hi, KT - 4, G_X + KT - 4, pair(2))
                if s == 1:
                    row_ms(NORM_Q, HALVES, TG)
                    chain(refine(NORM_Q, HALVES, fac[:, 0:HALVES]))
                    dve.tensor_scalar(scale_q[:, :], fac[:, 0:HALVES], SCALE, None, ALU.mult) \
                        .then_inc(rstd_ready, 1)
                    dve.wait_ge(rstd_ready, 3)
                if s == 5:
                    probs_out(cross, 0, 2 * S)
                    diagonals(1)
                if s == 6:
                    probs_out(cross + 1, 1, 2 * S)
                    head_lo(0)
                    cross_maxima(2)
                if s == 7:
                    head_lo(1)
                    diagonals(2)
            for s in range(TG * XP):
                n = P_XO + s + LEAD
                if s == 0:
                    probs_out(cross + 2, 2, 2 * S)
                    cross_maxima(3)
                if s == 2:
                    head_lo(3)
                lo(n, n % SLOTS)
                if s == 0:
                    diagonals(3)
                if s == 1:
                    probs_out(cross + 3, 3, 2 * S)
                    head_lo(2)
                if XO_PIECES[s][1] == 1:
                    c = XO_PIECES[s][0]
                    add_residual(P_XO + s + 1, pair(c % 2), c)
                if s in (4, 5, 7):
                    c = (4, 5, 7).index(s)
                    turned_lo(SPLIT_XO + c, t1_lo, t1_hi, 4 * c, G_FFN + 4 * c, pair(2 + c % 2))
            for s in range(CP):
                n = P_GATE0 + s + LEAD
                lo(n, n % SLOTS)
                if s == 1:
                    turned_lo(SPLIT_XO + TG - 1, t1_lo, t1_hi, KT - 4, G_FFN + KT - 4, pair(3))
                    row_ms(NORM_F, HALVES, TG)
                    refine(NORM_F, HALVES, rstd_f[:, :]).then_inc(rstd_ready, 1)
            dve.wait_ge(rstd_ready, 4)

            def hidden(i, n_end):
                dve.wait_ge(piece_used, n_end + SLOTS)
                dve.wait_ge(silu_out, i + 1)
                for hf in range(HALVES):
                    ins = dve.scalar_tensor_tensor(out=qk_tok[:, 1, hf, :], in0=pair(1)[:, hf, :],
                                                   scalar=rstd_f[:, hf:hf + 1],
                                                   in1=qk_tok[:, 0, hf, :],
                                                   op0=ALU.mult, op1=ALU.mult)
                ins.then_inc(h_ready, 1)

            def hidden_turned(i):
                dve.wait_ge(t_done, i + (T_H + 1))
                for b in range(2):
                    ins = dve.tensor_copy(
                        hT[:, bass.ds(4 * i + 2 * b, 2), :].rearrange("p k t -> p (k t)"),
                        pair(2)[:, b, :])
                ins.then_inc(t_out, 1)

            with dve.Fori(0, FC - 1) as i:
                for s in range(2 * CP):
                    n = P_FFN + 2 * CP * i + s
                    lo(n + LEAD, (s + LEAD) % SLOTS)
                    if s == CP - 1:
                        hidden(i, n + 1)
                    if s == CP + 2:
                        hidden_turned(i)
            for s in range(CP):
                n = P_FFN + 2 * CP * (FC - 1) + s
                lo(n + LEAD, (s + LEAD) % SLOTS)

            def h_rest(k, s):
                dve.wait_ge(h_hi_ready, k + 1)
                dve.tensor_tensor(h_lo[:, s, :], hT[:, bass.ds(k, 1), :].rearrange("p k t -> p (k t)"),
                                  h_hi[:, s, :].bitcast(F32), ALU.subtract).then_inc(h_split, 1)

            def down(i, first=False, last=False):
                for j in range(DOWN_STEP):
                    if j % 2 == 0 and not (first and j == 0) and not (last and j == DOWN_STEP - 2):
                        h_rest(SLOTS * i + j // 2 + 1, (j // 2 + 1) % SLOTS)
                    if not (last and j >= DOWN_STEP - LEAD):
                        lo(P_DOWN + LEAD + DOWN_STEP * i + j, (j + LEAD) % SLOTS)

            h_rest(0, 0)
            hidden(FC - 1, P_DOWN)
            h_rest(1, 1)
            hidden_turned(FC - 1)
            down(0, first=True)
            with dve.Fori(1, FK // SLOTS - 1) as i:
                down(i)
            down(FK // SLOTS - 1, last=True)

            def add_output(hf, c):
                x_part = x_tok[:, hf, c * W_GROUP:(c + 1) * W_GROUP]
                dve.wait_ge(bank_done, hf * TG + c + 1)
                dve.tensor_tensor(x_part, down_bank(hf, c), x_part, ALU.add).then_inc(resid, 1)

            def output_ms(hf):
                dve.wait_ge(ssq_ready, NORM_OUT + hf + 1)
                chain(dve.tensor_reduce(nt[:, 0:1], ssq[:, hf * TG:(hf + 1) * TG], AX.X, ALU.add))
                dve.tensor_scalar(ms[:, 0:1], nt[:, 0:1], 1.0 / D, EPS, ALU.mult, ALU.add) \
                    .then_inc(ms_ready, 1)

            def output_rstd(hf):
                refine(NORM_OUT + hf, 1, rstd_o[:, hf:hf + 1]).then_inc(rstd_o_ready, 1)
                dve.wait_ge(rstd_o_ready, hf + 1)

            def finish(hf, c):
                cols = slice(c * W_GROUP, (c + 1) * W_GROUP)
                dve.scalar_tensor_tensor(out=out_chunk(hf, c), in0=x_tok[:, hf, cols],
                                         scalar=rstd_o[:, hf:hf + 1], in1=gfin[:, cols],
                                         op0=ALU.mult, op1=ALU.mult).then_inc(dve_final, 1)

            dve.wait_ge(gfin_landed, 16)
            for c in range(TG):
                add_output(0, c)
            output_ms(0)
            add_output(1, 0)
            output_rstd(0)
            add_output(1, 1)
            add_output(1, 2)
            finish(0, 2)
            add_output(1, 3)
            finish(0, 3)
            output_ms(1)
            output_rstd(1)
            finish(1, 2)
            finish(1, 3)

        @block.tensor
        def _(pe):
            def product(n, banks, t_hi, t_lo, ready=None, hook=None):
                pieces = CP
                for j in range(pieces):
                    s = j % SLOTS
                    if ready is not None and j % 2 == 0:
                        pe.wait_ge(t_out, ready + j // 2 + 1)
                    pe.wait_ge(lo_ready, n + (j + 1 + SLOTS))
                    for kk in range(2):
                        k = 2 * j + kk
                        wh = w_hi[:, s, kk * W_GROUP:(kk + 1) * W_GROUP]
                        wl = w_lo[:, s, kk * W_GROUP:(kk + 1) * W_GROUP]
                        for hf in range(HALVES):
                            th = t_hi[:, k, hf * P:(hf + 1) * P]
                            tl = t_lo[:, k, hf * P:(hf + 1) * P]
                            first, last = k == 0, k == 2 * pieces - 1
                            pe.matmul(banks[:, hf, :], lhsT=th, rhs=wh, start=first, stop=False)
                            pe.matmul(banks[:, hf, :], lhsT=th, rhs=wl, start=False, stop=False)
                            mm = pe.matmul(banks[:, hf, :], lhsT=tl, rhs=wh, start=False, stop=last)
                    mm.then_inc(piece_used, 1)
                    if hook:
                        hook(j)

            def turn(banks, src, n_blocks=4):
                for kk in range(n_blocks):
                    for hf in range(HALVES):
                        at = (kk % 2) * S + hf * P
                        mm = pe.transpose(banks[:, kk // 2, at:at + P],
                                          src[:, hf, kk * P:(kk + 1) * P], ident[:, :])
                mm.then_inc(t_done, 1)

            pe.sem_inc(piece_used, SLOTS)
            pe.wait_ge(ident_ready, 1)
            pe.wait_ge(g_mix_landed, 16)
            pe.transpose(psum[:, 0, 0:KT], g_rows[0:KT, :], ident[0:KT, 0:KT]) \
                .then_inc(gains_turned, 1)
            for c in range(2):
                pe.wait_ge(x_landed[c], 16)
                turn(pair(2 + c), x_tok[:, :, c * W_GROUP:(c + 1) * W_GROUP])
            pe.wait_ge(gains_ready, 1)

            def z_scores(n, h):
                z = pair(2)[:, h % 2, :]
                k0, k1 = kT[:, 0, h, 0:P], kT[:, 0, h, P:S]
                q0, q1 = qT[:, 0, h, 0:P], qT[:, 0, h, P:S]
                pe.matmul(z[:, 0:P], lhsT=k0, rhs=q0, start=True, stop=True, skip_group_check=True)
                pe.matmul(z[:, P:2 * P], lhsT=k1, rhs=q1, start=False, stop=True,
                          skip_group_check=True)
                pe.matmul(z[:, 2 * P:3 * P], lhsT=k0, rhs=q1, start=False, stop=True,
                          skip_group_check=True).then_inc(z_done, 1)

            def reverse_sums(n, h):
                pe.wait_ge(sp_masked, n + 1)
                z, sp = pair(2)[:, h % 2, :], s_a[:, h % 2, :]
                pe.matmul(z[:, 0:2 * P], lhsT=ident_r[:, :], rhs=not_past[:, :], start=False,
                          stop=True, skip_group_check=True)
                pe.matmul(z[:, 0:3 * P], lhsT=neg_tri[:, :], rhs=sp[:, 0:3 * P], start=False,
                          stop=True, skip_group_check=True)
                pe.matmul(z[:, 2 * P:3 * P], lhsT=neg_one[:, :], rhs=sp[:, P:2 * P], start=False,
                          stop=True, skip_group_check=True).then_inc(cum_done, 1)

            def values(h, v):
                w, cols = s_c[:, h % 2, :], slice(h * HD, (h + 1) * HD)
                o = pair(3)
                pe.matmul(o[:, 0, cols], lhsT=w[:, 0:P], rhs=v[:, 0, cols], start=True, stop=True)
                pe.matmul(o[:, 1, cols], lhsT=w[:, 2 * P:3 * P], rhs=v[:, 0, cols], start=True,
                          stop=False)
                mm = pe.matmul(o[:, 1, cols], lhsT=w[:, P:2 * P], rhs=v[:, 1, cols], start=False,
                               stop=True)
                if h == HEADS - 1:
                    mm.then_inc(heads_done, 1)

            def scores(h):
                sc = pair(2)[:, 0, :]
                q0, q1 = qT[:, 1, h, 0:P], qT[:, 1, h, P:S]
                k0, k1 = kT[:, 1, h, 0:P], kT[:, 1, h, P:S]
                pe.matmul(sc[:, 0:P], lhsT=q0, rhs=k0, start=True, stop=True)
                pe.matmul(sc[:, P:2 * P], lhsT=q1, rhs=k1, start=True, stop=True)
                pe.matmul(sc[:, 2 * P:3 * P], lhsT=q1, rhs=k0, start=True, stop=True) \
                    .then_inc(s_done, 1)

            def turn_probs(n, h, blocks):
                pe.wait_ge(p_ready, n + 1)
                for b, src in enumerate(blocks):
                    mm = pe.transpose(pair(2)[:, 1, b * P:(b + 1) * P],
                                      s_b[:, h % 2, src * P:(src + 1) * P], ident[:, :])
                mm.then_inc(pt_done, 1)

            def mixer_hook(i, s):
                if i == 0 and s in (0, 2):
                    c = 2 + s // 2
                    pe.wait_ge(x_landed[c], 16)
                    pe.wait_ge(t_out, c - 1)
                    turn(pair(c), x_tok[:, :, c * W_GROUP:(c + 1) * W_GROUP])
                if i == 0 and s == 11:
                    pe.wait_ge(gains_landed, 16 * 5)
                    pe.wait_ge(t_out, TG)
                    pe.transpose(pair(3)[:, 0, 0:G_ROWS], g_rows[:, :],
                                 ident[0:G_ROWS, 0:G_ROWS]).then_inc(gains_turned, 1)
                if i == 0 and 19 <= s < 23:
                    c = s - 19
                    pe.wait_ge(mem_landed[c], 16)
                    pe.wait_ge(t_out, T_MEM if c == 0 else T_MEM + c - 1)
                    pe.wait_ge(gains_ready, 2)
                    turn(pair(2 + c % 2), o_tok[:, :, c * W_GROUP:(c + 1) * W_GROUP])
                if s == CP + 2:
                    pe.wait_ge(evac, 7 * i + 1)
                    pe.wait_ge(t_out, T_SB[i])
                    turn(pair(2), qk_tok[:, 0])
                if s == 2 * CP + 2:
                    pe.wait_ge(evac, 7 * i + 2)
                    pe.wait_ge(t_out, T_SB[i] + 1)
                    turn(pair(2), qk_tok[:, 1])
                for h in range(HEADS):
                    n = HEADS * i + h
                    if s == 3 * CP + 4 * h:
                        if h == 0:
                            pe.wait_ge(t_out, T_MB[i])
                            pe.wait_ge(consts_ready, 1)
                            pe.wait_ge(evac, 7 * i + 3)
                        if h >= 2:
                            pe.wait_ge(w_exp, n - 1)
                        z_scores(n, h)
                    if s == 3 * CP + 4 * h + 2:
                        reverse_sums(n, h)
                    if s == 3 * CP + 4 * h + 5:
                        if h == 0 and i:
                            pe.wait_ge(o_out, 2 * i)
                        pe.wait_ge(w_exp, n + 1)
                        values(h, v_tok[:, 0])
                    if s == 46 + 2 * h:
                        if h == 0:
                            pe.wait_ge(t_out, T_MB[i] + 2)
                        else:
                            pe.wait_ge(s_out, n)
                        scores(h)
                    if s == 48 + 2 * h:
                        if h >= 1:
                            pe.wait_ge(pt_out, n)
                        turn_probs(n, h, (0, 1, 2))
                    if s == min(50 + 2 * h, 55):
                        if h == 0:
                            pe.wait_ge(o_out, 2 * i + 1)
                            pe.wait_ge(evac, 7 * i + 6)
                        pe.wait_ge(pt_out, n + 1)
                        values(h, v_tok[:, 1])
                if s == 42:
                    pe.wait_ge(rotated, 2 * i + 1)
                    pe.wait_ge(w_exp, HEADS * i + HEADS)
                    turn(pair(2), qk_tok[:, 0])
                if s == 44:
                    pe.wait_ge(rotated, 2 * i + 2)
                    pe.wait_ge(t_out, T_MB[i] + 1)
                    turn(pair(2), qk_tok[:, 1])
                if i == GROUPS - 1 and s in (50, 53):
                    c = (s - 50) // 3
                    pe.wait_ge(t_out, T_O + c)
                    if c == 1:
                        pe.wait_ge(o_out, 2 * i + 1)
                    turn(pair(1), o_tok[:, :, c * W_GROUP:(c + 1) * W_GROUP])

            for i in range(GROUPS):
                for c in range(7):
                    if c >= 2:
                        pe.wait_ge(evac, 7 * i + c - 1)
                    elif i:
                        pe.wait_ge(evac, 7 * i)
                    th, tl = (t1_hi, t1_lo) if c == 6 else (t0_hi, t0_lo)
                    product(MIX_STEP * i + c * CP, pair(c % 2), th, tl,
                            ready=0 if i == 0 and c == 0 else None,
                            hook=lambda j: mixer_hook(i, c * CP + j))

            def turn_x(t, c, first, banks=pair(2)):
                pe.wait_ge(resid, first + c + 1)
                pe.wait_ge(t_out, t)
                turn(banks, x_tok[:, :, c * W_GROUP:(c + 1) * W_GROUP])

            def w_out_hook(c, j):
                if c == 0 and j in (0, 3):
                    g = 2 + j // 3
                    pe.wait_ge(t_out, T_O + g)
                    pe.wait_ge(pt_out, GROUPS * HEADS)
                    pe.wait_ge(o_out, g + 1)
                    turn(pair(2), o_tok[:, :, g * W_GROUP:(g + 1) * W_GROUP])
                if c == 0 and j == 6:
                    pe.wait_ge(evac, 7 * GROUPS)
                    pe.wait_ge(t_out, T_KX)
                    turn(pair(2), kvx_tok[:, 0])
                if c and j == 2:
                    turn_x(T_WOUT + c - 1, c - 1, 0)

            pe.wait_ge(t_out, T_O + 2)
            for c in range(TG):
                if c == 1:
                    pe.wait_ge(evac, 7 * GROUPS)
                if c >= 2:
                    pe.wait_ge(resid, c - 1)
                product(P_WOUT + c * CP, pair((c + 1) % 2), t0_hi, t0_lo,
                        ready=T_O if c == 0 else None, hook=lambda j: w_out_hook(c, j))

            cross = GROUPS * HEADS

            def cross_scores(h):
                pe.wait_ge(evac, 7 * GROUPS + h + 1)
                if h == 0:
                    pe.wait_ge(t_out, T_XO)
                else:
                    pe.wait_ge(p_ready, cross + h)
                for hf in range(HALVES):
                    mm = pe.matmul(pair(2)[:, 0, hf * S:(hf + 1) * S],
                                   lhsT=qT[:, 0, h, hf * P:(hf + 1) * P], rhs=kT[:, 0, h, :],
                                   start=True, stop=True)
                mm.then_inc(s_done, 1)

            def cross_probs(h):
                pe.wait_ge(diag_ready, h + 1)
                if h:
                    pe.wait_ge(pt_out, cross + h)
                for kt in range(2):
                    for hf in range(HALVES):
                        at = kt * S + hf * P
                        mm = pe.matmul(pair(2)[:, 1, at:at + P],
                                       lhsT=s_b[:, h % 2, hf * S + kt * P:hf * S + (kt + 1) * P],
                                       rhs=qk_tok[:, 0, h % 2, hf * P:(hf + 1) * P],
                                       start=True, stop=True)
                mm.then_inc(pt_done, 1)

            def cross_output(h):
                pe.wait_ge(pt_out, cross + h + 1)
                if h >= 2:
                    pe.wait_ge(o_out, 2 * GROUPS + h - 1)
                for kt in range(2):
                    mm = pe.matmul(pair(3)[:, h % 2, 0:S],
                                   lhsT=kvx_tok[:, 1, kt, h * HD:(h + 1) * HD],
                                   rhs=s_c[:, h % 2, kt * S:(kt + 1) * S],
                                   start=kt == 0, stop=kt == 1)
                mm.then_inc(heads_done, 1)

            pe.wait_ge(resid, TG - 1)
            for e, (h, half) in enumerate(XQ_PIECES):
                s = e % SLOTS
                pe.wait_ge(lo_ready, P_XQ + e + 1 + SLOTS)
                if half == 0:
                    pe.wait_ge(t_out, T_WOUT + 2)
                    if h >= 2:
                        pe.wait_ge(evac, 7 * GROUPS + h - 1)
                else:
                    pe.wait_ge(t_out, T_XO)
                q_bank = pair(1)[:, h % 2, 0:S]
                for kk in range(CP):
                    k = half * CP + kk
                    wh = w_hi[:, s, kk * P:(kk + 1) * P]
                    wl = w_lo[:, s, kk * P:(kk + 1) * P]
                    pe.matmul(q_bank, lhsT=wh, rhs=t1_hi[:, k, :], start=k == 0, stop=False)
                    pe.matmul(q_bank, lhsT=wh, rhs=t1_lo[:, k, :], start=False, stop=False)
                    mm = pe.matmul(q_bank, lhsT=wl, rhs=t1_hi[:, k, :], start=False,
                                   stop=k == KT - 1)
                mm.then_inc(piece_used, 1)
                if e == 0:
                    turn_x(T_WOUT + TG - 1, TG - 1, 0)
                if e == 3:
                    cross_scores(0)
                if e == 4:
                    cross_scores(1)
                    cross_probs(0)
                if e == 5:
                    cross_output(0)
                    cross_probs(1)
                if e == 6:
                    cross_scores(2)
                    cross_output(1)
                if e == 7:
                    cross_probs(2)
                    cross_scores(3)

            for e, (c, half) in enumerate(XO_PIECES):
                s = e % SLOTS
                if half == 0 and c >= 2:
                    pe.wait_ge(resid, TG + c - 1)
                if e in (0, 2):
                    pe.wait_ge(o_out, 2 * GROUPS + 2 * half + 2)
                pe.wait_ge(lo_ready, P_XO + e + 1 + SLOTS)
                for kk in range(2):
                    k = 2 * half + kk
                    wh = w_hi[:, s, kk * W_GROUP:(kk + 1) * W_GROUP]
                    wl = w_lo[:, s, kk * W_GROUP:(kk + 1) * W_GROUP]
                    for hf in range(HALVES):
                        th = t0_hi[:, k, hf * P:(hf + 1) * P]
                        tl = t0_lo[:, k, hf * P:(hf + 1) * P]
                        o = pair(c % 2)[:, hf, :]
                        pe.matmul(o, lhsT=th, rhs=wh, start=k == 0, stop=False)
                        pe.matmul(o, lhsT=th, rhs=wl, start=False, stop=False)
                        mm = pe.matmul(o, lhsT=tl, rhs=wh, start=False, stop=k == 3)
                mm.then_inc(piece_used, 1)
                if e == 0:
                    cross_output(2)
                    cross_probs(3)
                if e == 1:
                    cross_output(3)
                if e in (4, 5, 7):
                    t = (4, 5, 7).index(e)
                    turn_x(T_XO + max(t - 1, 0), t, TG, pair(2 + t % 2))
            product(P_GATE0, pair(0), t1_hi, t1_lo, ready=T_XO,
                    hook=lambda j: turn_x(T_XO + TG - 2, TG - 1, TG, pair(3)) if j == 1 else None)

            def turn_h(i):
                pe.wait_ge(h_ready, i + 2)
                pe.wait_ge(t_out, i + T_H)
                turn(pair(2), qk_tok[:, 1])

            pe.wait_ge(resid, 2 * TG)
            with pe.Fori(0, FC - 1) as i:
                pe.wait_ge(h_ready, i + 1)
                product(P_FFN + 2 * CP * i, pair(1), t1_hi, t1_lo)
                pe.wait_ge(silu_out, i + 1)
                product(P_FFN + 2 * CP * i + CP, pair(0), t1_hi, t1_lo,
                        hook=lambda j: turn_h(i) if j == 2 else None)
            pe.wait_ge(h_ready, FC)
            product(P_FFN + 2 * CP * (FC - 1), pair(1), t1_hi, t1_lo)

            def down_part(kk, s, j, q, hf, first=False, last=False):
                wh = w_hi[:, s, q * W_GROUP:(q + 1) * W_GROUP]
                wl = w_lo[:, s, q * W_GROUP:(q + 1) * W_GROUP]
                o = down_bank(hf, 2 * j + q)
                th, tl = (h[:, kk, hf * P:(hf + 1) * P] for h in (h_hi, h_lo))
                pe.matmul(o, lhsT=th, rhs=wh, start=first, stop=False, skip_group_check=True)
                pe.matmul(o, lhsT=th, rhs=wl, start=False, stop=False, skip_group_check=True)
                return pe.matmul(o, lhsT=tl, rhs=wh, start=False, stop=last, skip_group_check=True)

            def down(i, order, first=False):
                for e, (kk, j) in enumerate(order):
                    if j == 0:
                        pe.wait_ge(h_split, SLOTS * i + kk + 1)
                    if first and e == 0:
                        pe.wait_ge(silu_out, FC)
                    if first and e == 1:
                        turn_h(FC - 1)
                    if first and e == 2:
                        pe.wait_ge(t_out, T_END)
                    pe.wait_ge(lo_ready, DOWN_STEP * i + (P_DOWN + e + 1 + SLOTS))
                    for q in range(2):
                        for hf in range(HALVES):
                            mm = down_part(kk, e % SLOTS, j, q, hf, first=first and kk == 0)
                    mm.then_inc(piece_used, 1)

            down(0, DOWN_FIRST, first=True)
            with pe.Fori(1, FK // SLOTS - 1) as i:
                down(i, DOWN_ORDER)
            down(FK // SLOTS - 1, DOWN_ORDER[:-4])
            pe.wait_ge(h_split, FK)
            for hf in range(HALVES):
                for c in range(TG):
                    pe.wait_ge(lo_ready, P_END - 1 + c // 2 + SLOTS)
                    for kk in (SLOTS - 2, SLOTS - 1):
                        mm = down_part(kk, (2 * kk + c // 2) % SLOTS, c // 2, c % 2, hf,
                                       last=kk == SLOTS - 1)
                    mm.then_inc(bank_done, 1)


INPUTS = ["x", "mem", "positions", "g_mix", "w_in", "g_out_sb", "g_out_moba", "w_out", "g_xattn",
          "g_mem", "w_xq", "w_xkv", "w_xo", "g_ffn", "w_gate_up", "w_down", "g_final"]


def kernel(**inputs):
    import concourse.bacc as bacc
    from concourse.bass_utils import run_bass_kernel_spmd

    nc = bacc.Bacc("TRN2", target_bir_lowering=False, num_devices=1)
    arrays, args = {}, []
    for name in INPUTS:
        a = np.ascontiguousarray(inputs[name])
        arrays[f"in_{name}"] = a
        args.append(nc.dram_tensor(f"in_{name}", a.shape, mybir.dt.from_np(a.dtype),
                                   kind="ExternalInput").ap())
    out = nc.dram_tensor("out", (1, S, D), F32, kind="ExternalOutput").ap()
    build(nc, *args, out)
    return run_bass_kernel_spmd(nc, [arrays], core_ids=[0]).results[0]["out"]
```
